# Optimizing a Trainium2 kernel written in Bass

```python
import jax, jax.numpy as jnp
from jax import lax
import numpy as np

D_MODEL = 1024
BATCH = 1
SEQ = 256
DEPTH = 2
DEC_BATCH = 8
DEC_SEQ = 4
PAST_LEN = 2048
PAGE_SIZE = 128

N_A_LAYERS = DEPTH // 2
N_B_LAYERS = DEPTH - N_A_LAYERS
N_DENSE = (DEPTH + 1) // 2
N_MOE = DEPTH // 2
CONV_CH = D_MODEL
CONV_W = 31
HEAD_DIM = 64
N_HEADS = D_MODEL // HEAD_DIM
N_KV_HEADS = 4
GROUP = N_HEADS // N_KV_HEADS
WINDOW = 128
BLOCK = WINDOW
NUM_BUCKETS = 32
MAX_DISTANCE = 128
D_FF = 2816
N_EXPERTS = 8
TOP_K = 2
D_FF_EXPERT = 3584
EPS = 1e-6

kernel_name = 'yoco_conformer_swa_sink_moe_step'

def rms_norm(x, g):
    xf = x.astype(jnp.float32)
    y = xf * lax.rsqrt(jnp.mean(xf * xf, axis=-1, keepdims=True) + EPS)
    return (y * g.astype(jnp.float32)).astype(x.dtype)

def layer_norm(x, g, b):
    xf = x.astype(jnp.float32)
    mu = jnp.mean(xf, axis=-1, keepdims=True)
    xc = xf - mu
    var = jnp.mean(xc * xc, axis=-1, keepdims=True)
    y = xc * lax.rsqrt(var + EPS) * g.astype(jnp.float32) + b.astype(jnp.float32)
    return y.astype(x.dtype)

def t5_bucket(dist):
    n = np.maximum(dist, 0)
    max_exact = NUM_BUCKETS // 2
    large = max_exact + (np.log(np.maximum(n, 1) / max_exact) / np.log(MAX_DISTANCE / max_exact)
                         * (NUM_BUCKETS - max_exact)).astype(np.int32)
    large = np.minimum(large, NUM_BUCKETS - 1)
    return np.where(n < max_exact, n, large).astype(np.int32)

def rel_bias_heads(rel_bias, dist):
    q_len, s_len = dist.shape
    b = jnp.take(rel_bias, jnp.asarray(t5_bucket(dist)), axis=0).astype(jnp.float32)
    return jnp.transpose(b, (2, 0, 1)).reshape(N_KV_HEADS, GROUP, q_len, s_len)

def sink_attend(s, sinks, v, eq):
    sink = sinks.astype(jnp.float32).reshape(N_KV_HEADS, GROUP)[:, :, None, None]
    m = jnp.maximum(jnp.max(s, axis=-1, keepdims=True), sink)
    p = jnp.exp(s - m)
    denom = jnp.sum(p, axis=-1, keepdims=True) + jnp.exp(sink - m)
    return jnp.einsum(eq, (p / denom).astype(v.dtype), v)

def swa_prompt(q, k, v, sinks, rel_bias):
    B, T = q.shape[0], q.shape[1]
    nb = T // BLOCK
    qb = q.reshape(B, nb, BLOCK, N_KV_HEADS, GROUP, HEAD_DIM)

    def band(t):
        tb = t.reshape(B, nb, BLOCK, N_KV_HEADS, HEAD_DIM)
        prev = jnp.pad(tb, ((0, 0), (1, 0), (0, 0), (0, 0), (0, 0)))[:, :-1]
        return jnp.concatenate([prev, tb], axis=2)

    kb, vb = band(k), band(v)
    s = jnp.einsum('bnqkgd,bnskd->bnkgqs', qb, kb).astype(jnp.float32) * (HEAD_DIM ** -0.5)
    dist = np.arange(BLOCK)[:, None] + BLOCK - np.arange(2 * BLOCK)[None, :]
    valid = (dist >= 0) & (dist < WINDOW)
    first = (np.arange(nb)[:, None, None] == 0) & (np.arange(2 * BLOCK)[None, None, :] < BLOCK)
    valid = valid[None] & ~first
    s = s + rel_bias_heads(rel_bias, dist)
    s = jnp.where(valid[None, :, None, None], s, -jnp.inf)
    o = sink_attend(s, sinks, vb, 'bnkgqs,bnskd->bnqkgd')
    return o.reshape(B, T, N_HEADS * HEAD_DIM)

def swa_sample(q, kc, vc, sinks, rel_bias):
    Bd, S = q.shape[0], q.shape[1]
    s = jnp.einsum('bqkgd,bskd->bkgqs', q, kc).astype(jnp.float32) * (HEAD_DIM ** -0.5)
    dist = np.arange(S)[:, None] + WINDOW - np.arange(WINDOW + S)[None, :]
    valid = (dist >= 0) & (dist < WINDOW)
    s = s + rel_bias_heads(rel_bias, dist)
    s = jnp.where(valid, s, -jnp.inf)
    o = sink_attend(s, sinks, vc, 'bkgqs,bskd->bqkgd')
    return o.reshape(Bd, S, N_HEADS * HEAD_DIM)

def conv_module(x, prev, g_norm, w_pw1, b_pw1, w_dw, b_dw, g_ln, b_ln, w_pw2, b_pw2):
    h = rms_norm(x, g_norm)
    u = h @ w_pw1 + b_pw1
    a, gt = jnp.split(u, 2, axis=-1)
    u = a * jax.nn.sigmoid(gt)
    full = jnp.concatenate([prev, u], axis=1)
    c = lax.conv_general_dilated(full, w_dw[:, None, :], window_strides=(1,), padding='VALID',
                                 dimension_numbers=('NWC', 'WIO', 'NWC'),
                                 feature_group_count=CONV_CH) + b_dw
    c = jax.nn.silu(layer_norm(c, g_ln, b_ln))
    return x + c @ w_pw2 + b_pw2, full[:, -(CONV_W - 1):]

def dense_swiglu(x, g, w_gate, w_up, w_down):
    h = rms_norm(x, g)
    return x + (jax.nn.silu(h @ w_gate) * (h @ w_up)) @ w_down

def moe_swiglu(x, g, w_router, w_eg, w_eu, w_ed):
    h = rms_norm(x, g)
    hf = h.reshape(-1, D_MODEL)
    logits = (hf @ w_router).astype(jnp.float32)
    top_v, top_i = lax.top_k(logits, TOP_K)
    gates = jax.nn.softmax(top_v, axis=-1)
    combine = jnp.einsum('tk,tke->te', gates,
                         jax.nn.one_hot(top_i, N_EXPERTS, dtype=jnp.float32)).astype(h.dtype)
    y = jnp.zeros_like(hf)
    for e in range(N_EXPERTS):
        he = jax.nn.silu(hf @ w_eg[e]) * (hf @ w_eu[e])
        y = y + combine[:, e:e + 1] * (he @ w_ed[e])
    return x + y.reshape(x.shape)

def trunk(x, conv_prev, k_win, v_win, P):
    N, T = x.shape[0], x.shape[1]
    h = x
    conv_out = []
    k = v = kc = vc = None
    for l in range(DEPTH):
        if l < N_A_LAYERS:
            prev = (jnp.zeros((N, CONV_W - 1, CONV_CH), x.dtype) if conv_prev is None else conv_prev[l])
            h, st = conv_module(h, prev, P['g_conv_norm'][l], P['w_pw1'][l], P['b_pw1'][l],
                                P['w_dw'][l], P['b_dw'][l], P['g_ln'][l], P['b_ln'][l],
                                P['w_pw2'][l], P['b_pw2'][l])
            conv_out.append(st)
        else:
            j = l - N_A_LAYERS
            if j == 0:
                hk = rms_norm(h, P['g_kv_norm'])
                kv = (hk @ P['w_kv']).reshape(N, T, 2, N_KV_HEADS, HEAD_DIM)
                k = rms_norm(kv[:, :, 0], P['g_k_norm'])
                v = kv[:, :, 1]
                if k_win is not None:
                    kc = jnp.concatenate([k_win, k], axis=1)
                    vc = jnp.concatenate([v_win, v], axis=1)
            hq = rms_norm(h, P['g_attn_norm'][j])
            q = rms_norm((hq @ P['w_q'][j]).reshape(N, T, N_KV_HEADS, GROUP, HEAD_DIM), P['g_q_norm'][j])
            if k_win is None:
                o = swa_prompt(q, k, v, P['sinks'][j], P['rel_bias'])
            else:
                o = swa_sample(q, kc, vc, P['sinks'][j], P['rel_bias'])
            h = h + o @ P['w_o'][j]
        if l % 2 == 0:
            i = l // 2
            h = dense_swiglu(h, P['g_ffn_norm'][i], P['w_gate'][i], P['w_up'][i], P['w_down'][i])
        else:
            i = l // 2
            h = moe_swiglu(h, P['g_moe_norm'][i], P['w_router'][i], P['w_e_gate'][i],
                           P['w_e_up'][i], P['w_e_down'][i])
    if k_win is None:
        k_new, v_new = k[:, -WINDOW:], v[:, -WINDOW:]
    else:
        k_new, v_new = kc[:, -WINDOW:], vc[:, -WINDOW:]
    return h, jnp.stack(conv_out), k_new, v_new

def setup_inputs(seed: int = 0) -> dict:
    key = jax.random.key(seed)
    ks = iter(jax.random.split(key, 40))

    def nrm(shape, scale):
        return jax.random.normal(next(ks), shape, jnp.float32) * scale

    def gain(shape):
        return 1.0 + nrm(shape, 0.02)

    HD = N_HEADS * HEAD_DIM
    return {
        'x_prompt': nrm((BATCH, SEQ, D_MODEL), 1.0),
        'x_sample': nrm((DEC_BATCH, DEC_SEQ, D_MODEL), 1.0),
        'state_conv': nrm((N_A_LAYERS, DEC_BATCH, CONV_W - 1, CONV_CH), 0.5),
        'cache_k_win': nrm((DEC_BATCH, WINDOW, N_KV_HEADS, HEAD_DIM), 1.0),
        'cache_v_win': nrm((DEC_BATCH, WINDOW, N_KV_HEADS, HEAD_DIM), 1.0),
        'g_conv_norm': gain((N_A_LAYERS, D_MODEL)),
        'w_pw1': nrm((N_A_LAYERS, D_MODEL, 2 * CONV_CH), D_MODEL ** -0.5),
        'b_pw1': nrm((N_A_LAYERS, 2 * CONV_CH), 0.02),
        'w_dw': nrm((N_A_LAYERS, CONV_W, CONV_CH), CONV_W ** -0.5),
        'b_dw': nrm((N_A_LAYERS, CONV_CH), 0.02),
        'g_ln': gain((N_A_LAYERS, CONV_CH)),
        'b_ln': nrm((N_A_LAYERS, CONV_CH), 0.02),
        'w_pw2': nrm((N_A_LAYERS, CONV_CH, D_MODEL), CONV_CH ** -0.5),
        'b_pw2': nrm((N_A_LAYERS, D_MODEL), 0.02),
        'g_kv_norm': gain((D_MODEL,)),
        'w_kv': nrm((D_MODEL, 2 * N_KV_HEADS * HEAD_DIM), D_MODEL ** -0.5),
        'g_k_norm': gain((HEAD_DIM,)),
        'g_attn_norm': gain((N_B_LAYERS, D_MODEL)),
        'w_q': nrm((N_B_LAYERS, D_MODEL, HD), D_MODEL ** -0.5),
        'g_q_norm': gain((N_B_LAYERS, HEAD_DIM)),
        'sinks': nrm((N_B_LAYERS, N_HEADS), 1.0),
        'w_o': nrm((N_B_LAYERS, HD, D_MODEL), HD ** -0.5),
        'rel_bias': nrm((NUM_BUCKETS, N_HEADS), 0.5),
        'g_ffn_norm': gain((N_DENSE, D_MODEL)),
        'w_gate': nrm((N_DENSE, D_MODEL, D_FF), D_MODEL ** -0.5),
        'w_up': nrm((N_DENSE, D_MODEL, D_FF), D_MODEL ** -0.5),
        'w_down': nrm((N_DENSE, D_FF, D_MODEL), D_FF ** -0.5),
        'g_moe_norm': gain((N_MOE, D_MODEL)),
        'w_router': nrm((N_MOE, D_MODEL, N_EXPERTS), D_MODEL ** -0.5),
        'w_e_gate': nrm((N_MOE, N_EXPERTS, D_MODEL, D_FF_EXPERT), D_MODEL ** -0.5),
        'w_e_up': nrm((N_MOE, N_EXPERTS, D_MODEL, D_FF_EXPERT), D_MODEL ** -0.5),
        'w_e_down': nrm((N_MOE, N_EXPERTS, D_FF_EXPERT, D_MODEL), D_FF_EXPERT ** -0.5),
    }

def reference(x_prompt, x_sample, state_conv, cache_k_win, cache_v_win,
              g_conv_norm, w_pw1, b_pw1, w_dw, b_dw, g_ln, b_ln, w_pw2, b_pw2,
              g_kv_norm, w_kv, g_k_norm,
              g_attn_norm, w_q, g_q_norm, sinks, w_o, rel_bias,
              g_ffn_norm, w_gate, w_up, w_down,
              g_moe_norm, w_router, w_e_gate, w_e_up, w_e_down):
    P = dict(g_conv_norm=g_conv_norm, w_pw1=w_pw1, b_pw1=b_pw1, w_dw=w_dw, b_dw=b_dw,
             g_ln=g_ln, b_ln=b_ln, w_pw2=w_pw2, b_pw2=b_pw2,
             g_kv_norm=g_kv_norm, w_kv=w_kv, g_k_norm=g_k_norm,
             g_attn_norm=g_attn_norm, w_q=w_q, g_q_norm=g_q_norm, sinks=sinks, w_o=w_o,
             rel_bias=rel_bias,
             g_ffn_norm=g_ffn_norm, w_gate=w_gate, w_up=w_up, w_down=w_down,
             g_moe_norm=g_moe_norm, w_router=w_router, w_e_gate=w_e_gate,
             w_e_up=w_e_up, w_e_down=w_e_down)
    y_prompt, conv_p, k_p, v_p = trunk(x_prompt, None, None, None, P)
    y_sample, conv_s, k_s, v_s = trunk(x_sample, state_conv, cache_k_win, cache_v_win, P)
    return (y_prompt, y_sample, conv_p, conv_s, k_p, k_s, v_p, v_s)


_drawn_inputs = setup_inputs


def setup_inputs(seed=0):
    import zlib

    import numpy as np

    out = dict(_drawn_inputs(seed))
    spreads = {}
    factors = {'g_kv_norm': 8.09,
     'g_attn_norm': 27.073,
     'g_q_norm': 35.761,
     'sinks': 18.446,
     'g_ffn_norm': 3.633,
     'b_ln': 2.754,
     'g_moe_norm': 8.0}
    for name, (base, spread) in spreads.items():
        noise = np.random.default_rng([zlib.crc32(name.encode()), seed]).standard_normal(out[name].shape)
        drawn = base * np.exp(spread * noise) if base else spread * noise
        out[name] = __import__('jax').numpy.asarray(drawn.astype(out[name].dtype))
    for name, factor in factors.items():
        out[name] = (out[name] * factor).astype(out[name].dtype)
    return out
```

```python
from contextlib import ExitStack

import numpy as np

import concourse.bass as bass
from concourse import mybir

F32 = mybir.dt.float32
F32R = mybir.dt.float32r
I32 = mybir.dt.int32
ALU = mybir.AluOpType
ACT = mybir.ActivationFunctionType
AX = mybir.AxisListType

P = 128
D = 1024
KT_D = D // P
SEQ, NB, DS = 256, 8, 4
NS = NB * DS
T = SEQ + NS
TT = [(0, 128), (128, 128), (256, NS)]
CW = 31
HD, NH, NKV, GR = 64, 16, 4, 4
WIN = 128
FF, FE, NE, TOP_K = 2816, 3584, 8, 2
FT = FF // P
FH = FT // 2
EPS = 1e-6
MASKED = -1e30
UNIT = 2048
BPU = UNIT // P
CH = 256
NCH = FE // CH
UPE = 3 * NCH
LAND, RING = 6, 4
RAW = 4
SLOTS = 128
PASSES = -(-T // SLOTS)
GATES_AT = KT_D + 2
NOT_HERE = 4096.0

PE_CONV = 3
DVE_CONV = KT_D - PE_CONV
TAPS_BETWEEN = 8
TAPS = 8
GROUPS = [range(a, min(a + TAPS, CW)) for a in range(0, CW, TAPS)]

DOWN_UNITS = -(-KT_D * FH // BPU)
U_PW1 = 0
U_PW2 = U_PW1 + KT_D
U_GU = [U_PW2 + KT_D // 2, 0]
U_DOWN = [U_GU[0] + FH, 0]
U_GU[1] = U_DOWN[0] + DOWN_UNITS
U_DOWN[1] = U_GU[1] + FH
U_K = U_DOWN[1] + DOWN_UNITS
U_V = U_K + 1
U_Q = U_V + 1
U_O = U_Q + KT_D // 2
DENSE = U_O + KT_D // 2
DOWN_LAST = KT_D * FH - BPU * (DOWN_UNITS - 1)

VEC = {}
_at = 0
for _name, _n in (("g_conv", 8), ("b_a", 8), ("b_g", 8), ("b_dw", 8), ("g_ln", 8), ("b_ln", 8),
                  ("b_pw2", 8), ("g_ffn", 8), ("g_kv", 8), ("g_attn", 8), ("g_moe", 8),
                  ("g_k", 1), ("g_q", 1), ("sink_row", 1), ("sinks", NH), ("router", 8 * NE)):
    VEC[_name] = (_at, _at + _n)
    _at += _n
NVEC = _at
CON = {}
_at = 0
for _name, _n in (("ident", P), ("mean_d", P), ("mean_head", P), ("ones", P), ("before", P),
                  ("iota", SLOTS), ("own_new", 4 * NS), ("tie", NE * NE), ("eps", 1)):
    CON[_name] = (_at, _at + _n)
    _at += _n
NCON = _at
NREL = 33
RLEN = 384


def build(nc, io):
    with ExitStack() as ctx:
        def sb(name, shape, dt=F32, stack=ctx):
            return stack.enter_context(nc.sbuf_tensor(name, shape, dt))

        def sem(name):
            return ctx.enter_context(nc.semaphore(name))

        bank = [ctx.enter_context(nc.psum_tensor(f"bank{i}", [P, 512], F32)) for i in range(8)]
        STAT, MEAN = bank[7], bank[6]

        land = [sb(f"land{i}", [P, UNIT]) for i in range(LAND)]
        w_hi = [sb(f"w_hi{i}", [P, UNIT], F32R) for i in range(RING)]
        w_lo = [sb(f"w_lo{i}", [P, UNIT], F32R) for i in range(RING)]
        X = sb("X", [P, KT_D, T])
        vec = sb("vec", [P, NVEC])
        con = sb("con", [P, NCON])
        sq = sb("sq", [P, 2, T])
        stats = sb("stats", [P, 2, T])
        sd, rr = stats[:, 0, :], stats[:, 1, :]
        raw = sb("raw", [P, RAW, T])
        g_q8 = sb("g_q8", [P, 1])

        phases = [0]

        def phase(*tensors):
            phases[0] += 1
            with ExitStack() as stack:
                return [sb(f"{n}_{phases[0]}", s, dt, stack) for n, s, dt in tensors]

        conv_mem = phase(("H_hi", [P, KT_D, T], F32R), ("H_lo", [P, KT_D, T], F32R),
                         ("gate_s", [P, 2, T], F32), ("Up", [P, KT_D, SEQ + CW - 1], F32),
                         ("Us", [P, KT_D, NB, DS + CW - 1], F32), ("C", [P, KT_D, T], F32),
                         ("win", [P, NB, DS, CW], F32), ("odd", [P, SEQ], F32), ("w_dw", [P, KT_D, CW], F32),
                         ("diag", [P, len(GROUPS), TAPS, P], F32), ("relb", [NREL, NH], F32),
                         ("buckets", [NREL, RLEN], F32), ("rb", [NH, RLEN], F32))
        H_hi, H_lo, gate_s, Up, Us, C, win, odd, w_dw, diag, relb, buckets, rb = conv_mem
        _, _, gate_f, A_hi, A_lo = phase(
            ("H_hi", [P, KT_D, T], F32R), ("H_lo", [P, KT_D, T], F32R), ("gate_f", [P, 2, T], F32),
            ("A_hi", [P, FH + 1, T], F32R), ("A_lo", [P, FH + 1, T], F32R))
        attn = [("H_hi", [P, KT_D, T], F32R), ("H_lo", [P, KT_D, T], F32R),
                ("Q", [P, KT_D, T], F32), ("K", [P, 2, T], F32), ("V", [P, 3, 256], F32),
                ("KC", [P, 2, NB, WIN + DS], F32), ("VC", [WIN, NB, 256], F32),
                ("small", [P, 2, 32], F32)]
        _, _, Q, K, V, KC, VC, small, G_hi, G_lo = phase(
            *attn, ("G_hi", [P, KT_D, T], F32R), ("G_lo", [P, KT_D, T], F32R))
        bias, S, pT, SS, bias_o = phase(
            *attn, ("bias", [P, 2, GR, 2 * P], F32), ("S", [P, 2, GR * 2 * P], F32),
            ("pT", [P, 2, 512], F32), ("SS", [P, 4, WIN + NS], F32), ("bias_o", [P, 4, NB, DS], F32))[8:]
        raw_flat = raw[:].rearrange("p a t -> p (a t)")
        QZ = raw_flat[:, 0:16 * 64].rearrange("p (n b r) -> p n b r", n=2, b=NB)
        bias_c = raw_flat[:, 1024:1024 + WIN]
        bias_n = small[:, 0, 28:28 + DS]
        pTc = sq[:].rearrange("p a t -> p (a t)")[:, 0:512]
        pTn = stats[:].rearrange("p a t -> p (a t)")[0:NS, 0:512]
        moe = [("d_hi0", [P, UNIT], F32R), ("d_hi1", [P, UNIT], F32R),
               ("d_lo0", [P, UNIT], F32R), ("d_lo1", [P, UNIT], F32R),
               ("H_tok", [P, 3, D], F32), ("P01", [P, 3, SLOTS], F32), ("PG", [P, 3, SLOTS], F32),
               ("PT", [SLOTS, T], F32), ("slot_of", [P, 3, PASSES * NE + 1], F32),
               ("gate_of", [P, 3, PASSES * NE + 1], F32), ("lg", [P, 6, 3, NE], F32),
               ("cmp", [P, 2, 3, NE, NE], F32), ("top", [P, 16], F32), ("trips", [1, 2], I32)]
        (d_hi0, d_hi1, d_lo0, d_lo1, H_tok, P01, PG, PT, slot_of, gate_of, lg, cmp_, top, trips,
         xe_hi, xe_lo, silu_g, he, heT_hi, heT_lo, oe) = phase(
            *moe, ("xe_hi", [P, D], F32R), ("xe_lo", [P, D], F32R), ("silu_g", [P, CH], F32),
            ("he", [SLOTS, CH], F32), ("heT_hi", [P, CH], F32R), ("heT_lo", [P, CH], F32R),
            ("oe", [SLOTS, D], F32))
        Hm = phase(*moe, ("Hm", [P, KT_D, T], F32))[-1]
        d_hi, d_lo = [d_hi0, d_hi1], [d_lo0, d_lo1]

        def v(name, k=0, n=1):
            a = VEC[name][0] + k
            return vec[:, a:a + n]

        def c(name):
            return con[:, CON[name][0]:CON[name][1]]

        ident = c("ident")
        router = vec[:, VEC["router"][0]:VEC["router"][1]].rearrange("p (k e) -> p k e", k=KT_D)

        landed = [sem(f"landed{i}") for i in range(LAND)]
        hi_done = sem("hi_done")
        split = sem("split")
        used = sem("used")
        d_hi_done = sem("d_hi_done")
        d_split = sem("d_split")
        d_used = sem("d_used")
        in_vec, in_con, in_rel, in_state = (sem(n) for n in ("in_vec", "in_con", "in_rel", "in_state"))
        in_x = [sem(f"in_x{i}") for i in range(4)]
        sq_ready, sq_summed, sd_ready, rr_ready = (sem(n) for n in
                                                   ("sq_ready", "sq_summed", "sd_ready", "rr_ready"))
        raw_ready, h_hi_ready = sem("raw_ready"), sem("h_hi_ready")
        h_ready = [sem("h_ready_even"), sem("h_ready_odd")]
        dve_seq = sem("dve_seq")
        rel_sum, rb_ready, rb_stored = sem("rel_sum"), sem("rb_ready"), sem("rb_stored")
        pw1_done, sig_ready, u_ready = sem("pw1_done"), sem("sig_ready"), sem("u_ready")
        diag_ready, diag_used, cv_done, cp_ready = (sem(n) for n in ("diag_ready", "diag_used", "cv_done", "cp_ready"))
        in_dw, cs_ready = sem("in_dw"), sem("cs_ready")
        win_ready, c_ready, mean_ready, xc_ready, ln_ready = (
            sem(n) for n in ("win_ready", "c_ready", "mean_ready", "xc_ready", "ln_ready"))
        pw2_done, x_conv = sem("pw2_done"), sem("x_conv")
        gu_done, silu_ready, a_raw, a_hi_ready, a_ready = (
            sem(n) for n in ("gu_done", "silu_ready", "a_raw", "a_hi_ready", "a_ready"))
        down_done, x_ffn = sem("down_done"), sem("x_ffn")
        kq_done, kq_sq, kq_ms, kq_sd, kq_ready = (
            sem(n) for n in ("kq_done", "kq_sq", "kq_ms", "kq_sd", "kq_ready"))
        v_done, v_ready, in_kc, in_vc = sem("v_done"), sem("v_ready"), sem("in_kc"), sem("in_vc")
        in_bias = [sem("in_bias0"), sem("in_bias1")]
        sc_done, s_ready, nm_ready, es_arg, p_ready, pn_ready = (
            sem(n) for n in ("sc_done", "s_ready", "nm_ready", "es_arg", "p_ready", "pn_ready"))
        pT_done, pT_ready, pv_done, o_hi_ready, o_ready = (
            sem(n) for n in ("pT_done", "pT_ready", "pv_done", "o_hi_ready", "o_ready"))
        qz_ready, kc_ready, in_bias_s = sem("qz_ready"), sem("kc_ready"), sem("in_bias_s")
        wo_done, x_attn = sem("wo_done"), sem("x_attn")
        hm_ready, lg_done, lg_ready, htok_done, htok_ready, ex_ready, sel_ready, pos_done, route_ready = (
            sem(n) for n in ("hm_ready", "lg_done", "lg_ready", "htok_done", "htok_ready", "ex_ready",
                             "sel_ready", "pos_done", "route_ready"))
        P_ready, gathered, xe_hi_ready, xe_ready, PT_done, PT_ready = (
            sem(n) for n in ("P_ready", "gathered", "xe_hi_ready", "xe_ready", "PT_done", "PT_ready"))
        egu_done, esilu_ready, he_ready, heT_done, heT_hi_ready, heT_ready = (
            sem(n) for n in ("egu_done", "esilu_ready", "he_ready", "heT_done", "heT_hi_ready", "heT_ready"))
        eout_done, oe_ready, y_done, y_added = (
            sem(n) for n in ("eout_done", "oe_ready", "y_done", "y_added"))
        stored, conv_stored, kv_stored = sem("stored"), sem("conv_stored"), sem("kv_stored")

        STEPS = [(0, 0), (0, 1), (1, 0), (1, 1), None, (2, 0), (2, 1), (3, 0), (3, 1)]
        TURNS = [0]
        for _step in STEPS:
            TURNS.append(TURNS[-1] + (2 if _step is None else _step[1] + 1))
        owner = [i for i in range(len(STEPS)) for _ in range(TURNS[i + 1] - TURNS[i])]
        OUT_STEPS = [i for i, _step in enumerate(STEPS) if _step is None or _step[0] % 2 == 1]

        FIRST_UNITS = [(0, 0), (0, 1), (1, 0), (1, 1)]

        def sample_out(rows, ng, i):
            return bank[6][rows, 256 * ng:256 * ng + 256].rearrange("p (b i g t) -> p i g b t", b=NB, i=2, g=GR)[:, i]

        def sample_rows(dst, rows, ng):
            return dst[rows, GR * ng:GR * ng + GR, SEQ:T].rearrange("p g (b t) -> p g b t", b=NB)

        def h_count(a, k):
            return KT_D // 2 * a + k // 2 + 1

        def toeplitz(head, n_heads, rows, first, cols):
            per_head = P * RLEN
            return bass.AP(tensor=io["rel_rows"].tensor, offset=head * per_head + first,
                           ap=[[RLEN - 1, rows], [per_head, n_heads], [1, cols]])

        block = ctx.enter_context(nc.Block())

        @block.sync
        def _(sp):
            for i in range(4):
                sp.dma_start(X[:, 2 * i:2 * i + 2, :], io["x"][:, 2 * i:2 * i + 2, :]).then_inc(in_x[i], 16)
            for n in range(DENSE):
                if n >= LAND:
                    sp.wait_ge(split, n - LAND + 1)
                cols = UNIT
                if n in (U_DOWN[0] + DOWN_UNITS - 1, U_DOWN[1] + DOWN_UNITS - 1):
                    cols = DOWN_LAST * P
                sp.dma_start(land[n % LAND][:, 0:cols], io["w_dense"][n, :, 0:cols]).then_inc(landed[n % LAND], 16)

            def expert_pass(first_trip):
                with sp.Fori(0, NE) as e:
                    trip = sp.snap(first_trip + e)
                    for u in range(UPE):
                        ch, j = divmod(u, 3)
                        if u < LAND:
                            sp.wait_ge(split, DENSE - LAND + 1 + u)
                        if j < 2:
                            sp.wait_ge(split, trip * (2 * NCH) + (DENSE + 2 * (ch - 2) + j + 1))
                        else:
                            sp.wait_ge(d_split, trip * NCH + (ch + 1))
                        slot = (DENSE + u) % LAND
                        sp.dma_start(land[slot][:], io["w_expert"][bass.ds(e, 1), u, :, :].rearrange(
                            "a p n -> (a p) n")).then_inc(landed[slot], 16)

            expert_pass(0)
            sp.wait_ge(route_ready, 1)
            passes = sp.value_load(trips[0:1, 0:1], min_val=1, max_val=PASSES)
            with sp.If(passes > 1):
                with sp.Fori(1, passes) as p:
                    expert_pass(p * NE)
            n_trips = sp.value_load(trips[0:1, 1:2], min_val=NE, max_val=PASSES * NE)
            sp.wait_ge(y_added, n_trips * KT_D + KT_D)
            sp.dma_start(io["y"], X[:]).then_inc(stored, 16)
            sp.wait_ge(stored, 16)
            sp.wait_ge(conv_stored, 32)
            sp.wait_ge(kv_stored, 80)

        @block.tensor
        def _(pe):
            def mm3(out, w, x, start, stop, hi=None, lo=None):
                pe.matmul(out, w[0], x[0], start=start, stop=False)
                pe.matmul(out, w[0], x[1], start=False, stop=False)
                return pe.matmul(out, w[1], x[0], start=False, stop=stop)

            def wblock(n, i):
                a, b = i * P, (i + 1) * P
                return w_hi[n % RING][:, a:b], w_lo[n % RING][:, a:b]

            def H(k, a=0, b=T):
                return H_hi[:, k, a:b], H_lo[:, k, a:b]

            def wait_h(a, k):
                pe.wait_ge(h_ready[k % 2], h_count(a, k))

            def mean_part(q, k):
                pe.wait_ge(sq_ready, KT_D * q + k + 1)
                pe.matmul(STAT[:, 0:T], c("mean_d"), sq[:, k % 2, :], start=(k == 0),
                          stop=(k == KT_D - 1)).then_inc(sq_summed, 1)

            pe.wait_ge(in_con, 16)
            for k in range(KT_D):
                mean_part(0, k)
            for j in range(KT_D):
                pe.wait_ge(split, U_PW1 + j + 1)
                if j >= 2:
                    pe.wait_ge(u_ready, j - 1)
                for half in range(2):
                    out = bank[2 * (j % 2) + half][:, 0:T]
                    for k in range(KT_D):
                        if j == 0 and half == 0:
                            wait_h(0, k)
                        last = mm3(out, wblock(U_PW1 + j, KT_D * half + k), H(k), k == 0, k == KT_D - 1)
                last.then_inc(used, 1)
                if j == 0:
                    pe.wait_ge(in_rel, 32)
                    pe.matmul(bank[5][0:NH, 0:RLEN], relb[:, :], buckets[:, :], start=True, stop=True).then_inc(rel_sum, 1)
            for m, j in enumerate(range(DVE_CONV, KT_D)):
                if m == 0:
                    pe.wait_ge(rb_ready, 1)
                if m >= 2:
                    pe.wait_ge(cp_ready, m - 1)
                pe.wait_ge(u_ready, j + 1)
                for g, taps in enumerate(GROUPS):
                    pe.wait_ge(diag_ready, len(GROUPS) * m + g + 1)
                    for w in taps:
                        last = pe.matmul(bank[4 + m % 2][:, 0:SEQ], diag[:, g, w - taps[0], :], Up[:, j, w:w + SEQ],
                                         start=(w == 0), stop=(w == CW - 1))
                    last.then_inc(diag_used, 1)
                pe.wait_ge(diag_used, len(GROUPS) * (m + 1))
                pe.sem_inc(cv_done, 1)
            pe.wait_ge(cs_ready, KT_D)
            for k in range(KT_D):
                if k < DVE_CONV:
                    pe.wait_ge(c_ready, k + 1)
                else:
                    pe.wait_ge(cp_ready, k - DVE_CONV + 1)
                last = pe.matmul(MEAN[:, 0:T], c("mean_d"), C[:, k, :], start=(k == 0), stop=(k == KT_D - 1))
            last.then_inc(mean_ready, 1)
            for k in range(KT_D):
                mean_part(1, k)
            for d in range(KT_D):
                n = U_PW2 + d // 2
                pe.wait_ge(split, n + 1)
                if d >= 4:
                    pe.wait_ge(x_conv, d - 3)
                for k in range(KT_D):
                    if d == 0:
                        wait_h(1, k)
                    last = mm3(bank[d % 4][:, 0:T], wblock(n, KT_D * (d % 2) + k), H(k), k == 0, k == KT_D - 1)
                last.then_inc(pw2_done, 1)
                if d % 2:
                    pe.wait_ge(pw2_done, d + 1)
                    pe.sem_inc(used, 1)
                if d >= 2:
                    mean_part(2, d - 2)
            mean_part(2, KT_D - 2)
            mean_part(2, KT_D - 1)
            for half in range(2):
                for i in range(FH):
                    f = FH * half + i
                    n = U_GU[half] + i
                    pe.wait_ge(split, n + 1)
                    if f >= 2:
                        pe.wait_ge(a_raw, f - 1)
                    for part in range(2):
                        out = bank[2 * (f % 2) + part][:, 0:T]
                        for k in range(KT_D):
                            if f == 0 and part == 0:
                                wait_h(2, k)
                            last = mm3(out, wblock(n, KT_D * part + k), H(k), k == 0, k == KT_D - 1)
                    last.then_inc(used, 1)
                for d in range(KT_D):
                    if KT_D * half + d >= 2:
                        pe.wait_ge(x_ffn, KT_D * half + d - 1)
                    for i in range(FH):
                        f = FH * half + i
                        unit, blk = divmod(FH * d + i, BPU)
                        n = U_DOWN[half] + unit
                        pe.wait_ge(split, n + 1)
                        pe.wait_ge(a_ready, f + 1)
                        a = f % (FH + 1)
                        last = mm3(bank[4 + d % 2][:, 0:T], wblock(n, blk), (A_hi[:, a, :], A_lo[:, a, :]),
                                   i == 0, i == FH - 1)
                        if blk == BPU - 1 and i < FH - 1:
                            last.then_inc(used, 1)
                    last.then_inc(down_done, 1)
                    if blk == BPU - 1 or d == KT_D - 1:
                        pe.wait_ge(down_done, KT_D * half + d + 1)
                        pe.sem_inc(used, 1)
                    if half == 1 and d >= 2:
                        mean_part(3, d - 2)
            mean_part(3, KT_D - 2)
            mean_part(3, KT_D - 1)
            pe.wait_ge(split, U_K + 1)
            for t in range(2):
                for k in range(KT_D):
                    if t == 0:
                        wait_h(3, k)
                    last = mm3(bank[t][:, 0:T], wblock(U_K, KT_D * t + k), H(k), k == 0, k == KT_D - 1)
                last.then_inc(kq_done, 1)
            pe.wait_ge(kq_done, 2)
            pe.sem_inc(used, 1)
            pe.wait_ge(split, U_V + 1)
            for i, (t0, nt) in enumerate(TT):
                for k in range(KT_D):
                    a = k * 256
                    last = mm3(bank[2 + i // 2][0:nt, 256 * (i % 2):256 * (i % 2) + 256],
                               H(k, t0, t0 + nt), (w_hi[U_V % RING][:, a:a + 256], w_lo[U_V % RING][:, a:a + 256]),
                               k == 0, k == KT_D - 1)
            last.then_inc(v_done, 1)
            pe.wait_ge(v_done, 1)
            pe.sem_inc(used, 1)

            def head_mean(i):
                pe.wait_ge(kq_sq, i + 1)
                if i >= 2:
                    pe.wait_ge(kq_sd, i - 1)
                pe.matmul(bank[4 + i % 2][:, 0:T], c("mean_head"), sq[:, i % 2, :], start=True,
                          stop=True).then_inc(kq_ms, 1)

            head_mean(0)
            head_mean(1)
            pe.wait_ge(v_ready, 1)
            for t in range(KT_D):
                n = U_Q + t // 2
                pe.wait_ge(split, n + 1)
                pe.wait_ge(kq_ready, max(2, t - 1))
                for k in range(KT_D):
                    if t == 0:
                        wait_h(4, k)
                    last = mm3(bank[t % 4][:, 0:T], wblock(n, KT_D * (t % 2) + k), (G_hi[:, k, :], G_lo[:, k, :]),
                               k == 0, k == KT_D - 1)
                last.then_inc(kq_done, 1)
                if t % 2:
                    pe.wait_ge(kq_done, 2 + t + 1)
                    pe.sem_inc(used, 1)
                if t >= 1:
                    head_mean(2 + t - 1)
            head_mean(2 + KT_D - 1)

            def scores(s):
                if s >= 2:
                    pe.wait_ge(s_ready, s - 1)
                if STEPS[s] is None:
                    pe.wait_ge(qz_ready, 1)
                    for b in range(NB):
                        pair, half = divmod(b, 2)
                        at = (WIN + NS) * (pair % 2)
                        out = bank[2 * (s % 2) + pair // 2][64 * half:64 * half + 64, :]
                        for ng in range(2):
                            pe.matmul(out[:, at:at + WIN], QZ[:, ng, b, :], KC[:, ng, b, 0:WIN],
                                      start=(ng == 0), stop=(ng == 1))
                        for ng in range(2):
                            last = pe.matmul(out[:, at + WIN:at + WIN + NS], QZ[:, ng, b, :], K[:, ng, SEQ:T],
                                             start=(ng == 0), stop=(ng == 1))
                    last.then_inc(sc_done, 1)
                    return
                n, b = STEPS[s]
                ng, i = divmod(n, 2)
                rows = slice(HD * i, HD * i + HD)
                for g in range(GR):
                    q = Q[rows, GR * ng + g, P * b:P * b + P]
                    if b == 0:
                        last = pe.matmul(bank[2 * (s % 2)][:, P * g:P * g + P], q, K[rows, ng, 0:P],
                                         start=True, stop=True)
                    else:
                        last = pe.matmul(bank[2 * (s % 2) + g // 2][:, 2 * P * (g % 2):2 * P * (g % 2) + 2 * P],
                                         q, K[rows, ng, 0:2 * P], start=True, stop=True)
                last.then_inc(sc_done, 1)

            def attend(s):
                pe.wait_ge(pn_ready, s + 1)
                for m in range(TURNS[s], TURNS[s + 1]):
                    kb = m - TURNS[s]
                    if m >= 2:
                        pe.wait_ge(pT_ready, m - 1)
                    for g in range(GR):
                        out = bank[4 + m % 2][:, P * g:P * g + P]
                        if STEPS[s] is None:
                            src = SS[:, g, 0:WIN] if kb == 0 else SS[:, g, WIN:WIN + NS]
                            last = pe.transpose(out if kb == 0 else out[0:NS, :], src, ident)
                        else:
                            a = (g * (STEPS[s][1] + 1) + kb) * P
                            last = pe.transpose(out, S[:, s % 2, a:a + P], ident)
                    last.then_inc(pT_done, 1)
                if STEPS[s] is None:
                    pe.wait_ge(o_ready, OUT_STEPS.index(s))
                    pe.wait_ge(in_vc, 16)
                    pe.wait_ge(pT_ready, TURNS[s + 1])
                    for ng in range(2):
                        for b in range(NB):
                            a = P * (b // 2) + 64 * (b % 2) + 32 * ng
                            out = bank[6][:, 256 * ng + 32 * b:256 * ng + 32 * b + 32]
                            pe.matmul(out, VC[:, b, P * ng:P * ng + P], pTc[:, a:a + 32], start=True, stop=False)
                            last = pe.matmul(out, V[0:NS, 2, P * ng:P * ng + P], pTn[:, a:a + 32],
                                             start=False, stop=True)
                    last.then_inc(pv_done, 1)
                    return
                n, b = STEPS[s]
                i = n % 2
                if n == 2:
                    pe.wait_ge(o_ready, 3 if b == 0 else 2)
                for kb in range(b + 1):
                    m = TURNS[s] + kb
                    pe.wait_ge(pT_ready, m + 1)
                    last = pe.matmul(bank[6 + b][HD * i:HD * i + HD, :], V[:, kb, HD * n:HD * n + HD],
                                     pT[:, m % 2, :], start=(kb == 0), stop=(kb == b))
                last.then_inc(pv_done, 1)

            pe.wait_ge(kq_ready, 2 + KT_D)
            scores(0)
            scores(1)
            for s in range(len(STEPS)):
                if s >= 1 and s + 1 < len(STEPS):
                    scores(s + 1)
                attend(s)
            pe.wait_ge(o_ready, len(OUT_STEPS))
            for d in range(KT_D):
                n = U_O + d // 2
                pe.wait_ge(split, n + 1)
                if d >= 4:
                    pe.wait_ge(x_attn, d - 3)
                for k in range(KT_D):
                    last = mm3(bank[d % 4][:, 0:T], wblock(n, KT_D * (d % 2) + k), H(k), k == 0, k == KT_D - 1)
                last.then_inc(wo_done, 1)
                if d % 2:
                    pe.wait_ge(wo_done, d + 1)
                    pe.sem_inc(used, 1)
                if d >= 2:
                    mean_part(4, d - 2)
            pe.wait_ge(kv_stored, 80)
            pe.sem_inc(d_used, 2)
            mean_part(4, KT_D - 2)
            mean_part(4, KT_D - 1)

            pe.wait_ge(hm_ready, KT_D)
            for i, (t0, nt) in enumerate(TT):
                for k in range(KT_D):
                    last = pe.matmul(bank[0][0:nt, NE * i:NE * i + NE], Hm[:, k, t0:t0 + nt], router[:, k, :],
                                     start=(k == 0), stop=(k == KT_D - 1))
            last.then_inc(lg_done, 1)
            for i, (t0, nt) in enumerate(TT):
                for h in range(2):
                    for k in range(4):
                        last = pe.transpose(bank[1 + 2 * i + h][0:nt, P * k:P * k + P],
                                            Hm[:, 4 * h + k, t0:t0 + nt], ident)
                    last.then_inc(htok_done, 1)
            sel = lg[:, 1]
            pe.wait_ge(sel_ready, 1)
            for i, (t0, nt) in enumerate(TT):
                for j in range(i + 1):
                    m = TT[j][1]
                    pe.matmul(bank[0][0:nt, 32 + NE * i:32 + NE * i + NE], (c("before") if j == i else c("ones"))[0:m, 0:nt],
                              sel[0:m, j, :], start=(j == 0), stop=(j == i))
            for j in range(3):
                m = TT[j][1]
                last = pe.matmul(bank[0][:, 64:64 + NE], c("ones")[0:m, :], sel[0:m, j, :], start=(j == 0), stop=(j == 2))
            last.then_inc(pos_done, 1)
            pe.wait_ge(route_ready, 1)
            n_trips = pe.value_load(trips[0:1, 1:2], min_val=NE, max_val=PASSES * NE)

            def gather(h):
                for k in range(4):
                    for j, (t0, nt) in enumerate(TT):
                        last = pe.matmul(bank[4 + h][:, P * k:P * k + P],
                                         H_tok[0:nt, j, (4 * h + k) * P:(4 * h + k + 1) * P],
                                         P01[0:nt, j, :], start=(j == 0), stop=(j == 2))
                last.then_inc(gathered, 1)

            def turn_gates():
                for j, (t0, nt) in enumerate(TT):
                    last = pe.transpose(bank[7][:, t0:t0 + nt], PG[0:nt, j, :], ident[0:nt, 0:nt])
                last.then_inc(PT_done, 1)

            pe.wait_ge(htok_ready, 6)
            pe.wait_ge(P_ready, 1)
            gather(0)
            gather(1)

            def back(trip, k):
                pe.wait_ge(oe_ready, trip * 2 + 2)
                pe.wait_ge(PT_ready, trip + 1)
                if k:
                    pe.wait_ge(y_added, trip * KT_D + k)
                pe.matmul(bank[7][:, 0:T], oe[:, P * k:P * k + P], PT[:, :], start=True, stop=True).then_inc(y_done, 1)

            with pe.Fori(0, n_trips) as trip:
                def gate_up(ch, h):
                    n = DENSE + 2 * ch + h
                    pe.wait_ge(split, trip * (2 * NCH) + n + 1)
                    for k in range(4):
                        kk = 4 * h + k
                        last = mm3(bank[ch % 2][:, :], (xe_hi[:, kk * P:kk * P + P], xe_lo[:, kk * P:kk * P + P]),
                                   (w_hi[n % RING][:, 512 * k:512 * k + 512], w_lo[n % RING][:, 512 * k:512 * k + 512]),
                                   kk == 0, kk == KT_D - 1)
                    last.then_inc(used, 1)

                def turn(ch):
                    pe.wait_ge(he_ready, trip * NCH + ch + 1)
                    for k in range(2):
                        last = pe.transpose(bank[6][:, P * k:P * k + P], he[:, P * k:P * k + P], ident)
                    last.then_inc(heT_done, 1)

                def down(ch):
                    pe.wait_ge(heT_ready, trip * NCH + ch + 1)
                    if ch == 0:
                        pe.wait_ge(oe_ready, trip * 2 + 2)
                    pe.wait_ge(d_split, trip * NCH + ch + 1 + 2)
                    for h in range(2):
                        for k in range(2):
                            a = D * k + 512 * h
                            last = mm3(bank[2 + h][:, :], (heT_hi[:, P * k:P * k + P], heT_lo[:, P * k:P * k + P]),
                                       (d_hi[ch % 2][:, a:a + 512], d_lo[ch % 2][:, a:a + 512]),
                                       ch == 0 and k == 0, ch == NCH - 1 and k == 1)
                    last.then_inc(d_used, 1)

                pe.wait_ge(xe_ready, (trip + 1) * 2)
                gate_up(0, 0)
                gate_up(0, 1)
                for ch in range(NCH):
                    if ch + 1 < NCH:
                        gate_up(ch + 1, 0)
                        turn(ch)
                        gate_up(ch + 1, 1)
                    else:
                        with pe.If(trip < n_trips - 1):
                            pe.wait_ge(P_ready, trip + 2)
                            gather(0)
                        turn(ch)
                        with pe.If(trip < n_trips - 1):
                            gather(1)
                    down(ch)
                    if 1 <= ch <= KT_D:
                        back(trip, ch - 1)
                    if ch == GATES_AT:
                        pe.wait_ge(y_added, trip * KT_D + KT_D)
                        turn_gates()
            for k in range(KT_D):
                back(n_trips, k)

        @block.scalar
        def _(act):
            act.dma_start(con[:], io["con"]).then_inc(in_con, 16)
            act.dma_start(vec[:], io["vec"]).then_inc(in_vec, 16)
            act.dma_start(w_dw[:], io["w_dw"]).then_inc(in_dw, 16)
            act.dma_start(relb[:], io["relb"]).then_inc(in_rel, 16)
            act.dma_start(buckets[:], io["buckets"]).then_inc(in_rel, 16)
            act.dma_start(Us[:], io["state"]).then_inc(in_state, 16)

            n_hi = 0

            def hi_to(m):
                nonlocal n_hi
                while n_hi < min(m, DENSE):
                    n = n_hi
                    act.wait_ge(landed[n % LAND], 16 * (n // LAND + 1))
                    if n >= RING:
                        act.wait_ge(used, n - RING + 1)
                    cols = DOWN_LAST * P if n in (U_DOWN[0] + DOWN_UNITS - 1, U_DOWN[1] + DOWN_UNITS - 1) else UNIT
                    act.copy(w_hi[n % RING][:, 0:cols], land[n % LAND][:, 0:cols]).then_inc(hi_done, 1)
                    n_hi += 1

            def square(q, src, k):
                if KT_D * q + k >= 2:
                    act.wait_ge(sq_summed, KT_D * q + k - 1)
                act.activation(sq[:, k % 2, :], src[:, k, :], ACT.Square).then_inc(sq_ready, 1)

            def root(q):
                act.wait_ge(sq_summed, KT_D * (q + 1))
                act.activation(sd[:], STAT[:, 0:T], ACT.Sqrt, bias=c("eps")).then_inc(sd_ready, 1)

            def h_hi(a, dst):
                for k in range(KT_D):
                    m = KT_D * a + k
                    act.wait_ge(raw_ready, m + 1)
                    act.copy(dst[:, k, :], raw[:, m % RAW, :]).then_inc(h_hi_ready, 1)

            act.wait_ge(in_con, 16)
            for k in range(KT_D):
                act.wait_ge(in_x[k // 2], 16)
                square(0, X, k)
            root(0)
            hi_to(1)
            h_hi(0, H_hi)
            hi_to(RING)
            act.wait_ge(in_vec, 16)
            for j in range(KT_D):
                hi_to(j + RING)
                act.wait_ge(used, U_PW1 + j + 1)
                if j >= 2:
                    act.wait_ge(u_ready, j - 1)
                act.activation(gate_s[:, j % 2, :], bank[2 * (j % 2) + 1][:, 0:T], ACT.Sigmoid,
                               bias=v("b_g", j)).then_inc(sig_ready, 1)
            hi_to(U_PW2 + RING)
            for m, j in enumerate(range(DVE_CONV, KT_D)):
                act.wait_ge(cv_done, m + 1)
                act.activation(C[:, j, 0:SEQ], bank[4 + m % 2][:, 0:SEQ], ACT.Identity,
                               bias=v("b_dw", j)).then_inc(cp_ready, 1)
            for k in range(KT_D):
                act.wait_ge(xc_ready, k + 1)
                square(1, C, k)
            root(1)

            def ln_hi(k):
                act.wait_ge(raw_ready, KT_D + k + 1)
                act.copy(H_hi[:, k, :], raw[:, (KT_D + k) % RAW, :]).then_inc(h_hi_ready, 1)

            for k in range(KT_D):
                m = KT_D + k
                act.wait_ge(ln_ready, k + 1)
                act.wait_ge(h_ready[m % 2], m // 2 - 1)
                act.activation(raw[:, m % RAW, :], C[:, k, :], ACT.Silu, bias=v("b_ln", k)).then_inc(raw_ready, 1)
                if k >= 1:
                    ln_hi(k - 1)
            ln_hi(KT_D - 1)
            for k in range(KT_D):
                act.wait_ge(x_conv, k + 1)
                square(2, X, k)
                if k % 2 and k < KT_D - 1:
                    hi_to(U_PW2 + RING + k // 2 + 1)
            root(2)
            h_hi(2, H_hi)
            hi_to(U_GU[0] + RING)
            act.wait_ge(conv_stored, 32)
            for half in range(2):
                for i in range(FH):
                    f = FH * half + i
                    hi_to(U_GU[half] + i + RING)
                    act.wait_ge(used, U_GU[half] + i + 1)
                    act.activation(gate_f[:, f % 2, :], bank[2 * (f % 2)][:, 0:T], ACT.Silu).then_inc(silu_ready, 1)
                    act.wait_ge(a_raw, f + 1)
                    if half == 1:
                        act.wait_ge(down_done, KT_D)
                    act.copy(A_hi[:, f % (FH + 1), :], raw[:, f % RAW, :]).then_inc(a_hi_ready, 1)
                for d in range(KT_D):
                    hi_to(U_DOWN[half] + min(DOWN_UNITS, FH * d // BPU) + RING)
                    if half == 1:
                        act.wait_ge(x_ffn, KT_D + d + 1)
                        square(3, X, d)
                if half == 0:
                    hi_to(U_GU[1] + 3)
            root(3)
            act.dma_start(KC[:], io["kc"]).then_inc(in_kc, 16)
            act.dma_start(VC[:], io["vc"]).then_inc(in_vc, 16)
            h_hi(3, H_hi)
            hi_to(U_K + RING)
            h_hi(4, G_hi)

            def head_square(i):
                src = bank[i] if i < 2 else bank[(i - 2) % 4]
                act.wait_ge(kq_done, i + 1)
                if i >= 2:
                    act.wait_ge(kq_ms, i - 1)
                act.activation(sq[:, i % 2, :], src[:, 0:T], ACT.Square).then_inc(kq_sq, 1)

            def head_root(i):
                act.wait_ge(kq_ms, i + 1)
                if i >= 1:
                    act.wait_ge(kq_ready, i)
                act.activation(sd[:], bank[4 + i % 2][:, 0:T], ACT.Sqrt, bias=c("eps")).then_inc(kq_sd, 1)

            head_square(0)
            head_square(1)
            hi_to(U_V + RING)
            head_root(0)
            head_root(1)
            for t in range(KT_D):
                hi_to(U_Q + t // 2 + RING)
                head_square(2 + t)
                head_root(2 + t)
            act.wait_ge(rb_stored, 16)
            for n in range(2):
                act.dma_start(bias[:, n], toeplitz(GR * n, GR, P, P - 1, 2 * P)).then_inc(in_bias[n], 16)
            act.wait_ge(h_ready[0], 5 * KT_D // 2)
            act.wait_ge(h_ready[1], 5 * KT_D // 2)
            per_head = P * RLEN
            for two in range(2):
                for dst, first, cols in ((bias_c, P - 1, WIN), (bias_n, 2 * P - 1, DS)):
                    act.dma_start(dst[64 * two:64 * two + 64, :],
                                  bass.AP(tensor=io["rel_rows"].tensor, offset=first,
                                          ap=[[per_head, NH], [RLEN - 1, DS], [1, cols]])).then_inc(in_bias_s, 16)

            def exps(s):
                sm = small[:, s % 2, :]
                act.wait_ge(nm_ready, s + 1)
                for g in range(GR):
                    if STEPS[s] is None:
                        part = SS[:, g, :]
                    else:
                        w = (STEPS[s][1] + 1) * P
                        part = S[:, s % 2, w * g:w * g + w]
                    act.activation(part, part, ACT.Exp, bias=sm[:, 4 + g:5 + g], accum_out=sm[:, 8 + g:9 + g])
                act.wait_ge(es_arg, s + 1)
                act.activation(sm[:, 16:20], sm[:, 12:16], ACT.Exp).then_inc(p_ready, 1)
                if STEPS[s] in ((0, 1), (1, 1)):
                    n = STEPS[s][0]
                    act.wait_ge(s_ready, s + 1)
                    act.dma_start(bias[:, n], toeplitz(GR * (n + 2), GR, P, P - 1, 2 * P)).then_inc(in_bias[n], 16)

            def o_hi(s):
                act.wait_ge(pv_done, s + 1)
                if STEPS[s] is None:
                    for ng in range(2):
                        for i in range(2):
                            rows = slice(HD * i, HD * i + HD)
                            last = act.copy(sample_rows(H_hi, rows, ng), sample_out(rows, ng, i))
                else:
                    n, b = STEPS[s]
                    ng = n // 2
                    last = act.copy(H_hi[:, GR * ng:GR * ng + GR, P * b:P * b + P],
                                    bank[6 + b][:, :].rearrange("p (g q) -> p g q", g=GR))
                last.then_inc(o_hi_ready, 1)

            exps(0)
            for s in range(len(STEPS)):
                if s + 1 < len(STEPS):
                    exps(s + 1)
                if s == 0:
                    hi_to(DENSE)
                if s - 1 in OUT_STEPS:
                    o_hi(s - 1)
                for m in range(TURNS[s], TURNS[s + 1]):
                    act.wait_ge(pT_done, m + 1)
                    if m >= 2:
                        act.wait_ge(pv_done, owner[m - 2] + 1)
                    if STEPS[s] is not None:
                        act.copy(pT[:, m % 2, :], bank[4 + m % 2][:, :]).then_inc(pT_ready, 1)
                    elif m == TURNS[s]:
                        act.copy(pTc, bank[4 + m % 2][:, :]).then_inc(pT_ready, 1)
                    else:
                        act.copy(pTn, bank[4 + m % 2][0:NS, :]).then_inc(pT_ready, 1)
            o_hi(len(STEPS) - 1)

            def expert_hi(trip, ch, j):
                u = 3 * ch + j
                act.wait_ge(landed[(DENSE + u) % LAND], trip * (16 * UPE // LAND) + 16 * ((DENSE + u) // LAND + 1))
                if j < 2:
                    n = DENSE + 2 * ch + j
                    act.wait_ge(used, trip * (2 * NCH) + n - RING + 1)
                    act.copy(w_hi[n % RING][:], land[(DENSE + u) % LAND][:]).then_inc(hi_done, 1)
                else:
                    act.wait_ge(d_used, trip * NCH + ch + 1)
                    act.copy(d_hi[ch % 2][:], land[(DENSE + u) % LAND][:]).then_inc(d_hi_done, 1)

            for k in range(KT_D):
                act.wait_ge(x_attn, k + 1)
                square(4, X, k)
                if k % 2 and k < KT_D - 1:
                    expert_hi(0, *FIRST_UNITS[k // 2])
            root(4)
            expert_hi(0, *FIRST_UNITS[3])
            expert_hi(0, 0, 2)
            act.wait_ge(lg_ready, 1)
            act.activation(lg[:, 2], lg[:, 3], ACT.Exp).then_inc(ex_ready, 1)
            act.wait_ge(route_ready, 1)
            n_trips = act.value_load(trips[0:1, 1:2], min_val=NE, max_val=PASSES * NE)

            def xe_split(first, h):
                act.wait_ge(gathered, first + h + 1)
                act.copy(xe_hi[:, 512 * h:512 * h + 512], bank[4 + h][:, :]).then_inc(xe_hi_ready, 1)

            xe_split(0, 0)
            xe_split(0, 1)
            with act.Fori(0, n_trips) as trip:
                for ch in range(NCH):
                    act.wait_ge(used, trip * (2 * NCH) + DENSE + 2 * ch + 2)
                    act.activation(silu_g[:], bank[ch % 2][:, 0:CH], ACT.Silu).then_inc(esilu_ready, 1)
                    if ch == GATES_AT + 1:
                        act.wait_ge(PT_done, trip + 1)
                        act.copy(PT[:, :], bank[7][:, 0:T]).then_inc(PT_ready, 1)
                    if ch + 1 < NCH:
                        expert_hi(trip, ch + 1, 2)
                    else:
                        with act.If(trip < n_trips - 1):
                            xe_split((trip + 1) * 2, 0)
                    act.wait_ge(heT_done, trip * NCH + ch + 1)
                    act.wait_ge(d_used, trip * NCH + ch + 2)
                    act.copy(heT_hi[:], bank[6][:, 0:CH]).then_inc(heT_hi_ready, 1)
                    if ch + 2 < NCH:
                        expert_hi(trip, ch + 2, 0)
                        expert_hi(trip, ch + 2, 1)
                    elif ch + 2 == NCH:
                        with act.If(trip < n_trips - 1):
                            expert_hi(trip, ch + 2, 0)
                            expert_hi(trip, ch + 2, 1)
                    else:
                        with act.If(trip < n_trips - 1):
                            xe_split((trip + 1) * 2, 1)
                            expert_hi(trip, ch + 2, 0)
                            expert_hi(trip, NCH, 2)
                            expert_hi(trip, ch + 2, 1)
                act.wait_ge(d_used, trip * NCH + NCH + 2)
                act.copy(oe[:, 0:512], bank[2][:, :]).then_inc(oe_ready, 1)

        @block.vector
        def _(dve):
            count = [0]

            def seq(ins):
                count[0] += 1
                ins.then_inc(dve_seq, 1)
                dve.wait_ge(dve_seq, count[0])

            n_lo = 0

            def lo_to(m):
                nonlocal n_lo
                while n_lo < min(m, DENSE):
                    n = n_lo
                    cols = DOWN_LAST * P if n in (U_DOWN[0] + DOWN_UNITS - 1, U_DOWN[1] + DOWN_UNITS - 1) else UNIT
                    dve.wait_ge(hi_done, n + 1)
                    dve.tensor_tensor(w_lo[n % RING][:, 0:cols], land[n % LAND][:, 0:cols],
                                      w_hi[n % RING][:, 0:cols].bitcast(F32), ALU.subtract).then_inc(split, 1)
                    n_lo += 1

            def inverse_root(q):
                dve.wait_ge(sd_ready, q + 1)
                dve.reciprocal(rr[:], sd[:]).then_inc(rr_ready, 1)
                dve.wait_ge(rr_ready, q + 1)

            def h_lo_odd(a, k, hi, lo):
                m = KT_D * a + k
                dve.wait_ge(h_hi_ready, m + 1)
                dve.tensor_tensor(lo[:, k, :], raw[:, m % RAW, :], hi[:, k, :].bitcast(F32),
                                  ALU.subtract).then_inc(h_ready[1], 1)

            def normed(a, gain, hi, lo):
                for k in range(KT_D):
                    m = KT_D * a + k
                    if m >= RAW:
                        dve.wait_ge(h_ready[m % 2], m // 2 - 1)
                    dve.scalar_tensor_tensor(out=raw[:, m % RAW, :], in0=X[:, k, :], scalar=v(gain, k), in1=rr[:],
                                             op0=ALU.mult, op1=ALU.mult).then_inc(raw_ready, 1)
                    if k % 2 and k >= 3:
                        h_lo_odd(a, k - 2, hi, lo)
                h_lo_odd(a, KT_D - 1, hi, lo)

            seq(dve.memset(Up[:, :, 0:CW - 1], 0.0))
            dve.wait_ge(in_vec, 16)
            seq(dve.tensor_scalar(g_q8[:], v("g_q"), HD ** -0.5, None, ALU.mult))
            inverse_root(0)
            lo_to(1)
            normed(0, "g_conv", H_hi, H_lo)
            lo_to(RING)

            tap_done = {}

            def tap(j, w):
                acc = odd[:] if w % 2 else C[:, j, 0:SEQ]
                x = Up[:, j, w:w + SEQ]
                if w == 0:
                    dve.wait_ge(u_ready, j + 1)
                    ins = dve.tensor_scalar(acc, x, w_dw[:, j, w:w + 1], v("b_dw", j), ALU.mult, ALU.add)
                elif w == 1:
                    if j >= 1:
                        dve.wait_ge(c_ready, j)
                    ins = dve.tensor_scalar(acc, x, w_dw[:, j, w:w + 1], None, ALU.mult)
                else:
                    dve.wait_ge(dve_seq, tap_done[w % 2])
                    ins = dve.scalar_tensor_tensor(out=acc, in0=x, scalar=w_dw[:, j, w:w + 1], in1=acc,
                                                   op0=ALU.mult, op1=ALU.add)
                ins.then_inc(dve_seq, 1)
                count[0] += 1
                tap_done[w % 2] = count[0]
                if w == CW - 1:
                    dve.wait_ge(dve_seq, count[0])
                    dve.tensor_tensor(C[:, j, 0:SEQ], C[:, j, 0:SEQ], odd[:], ALU.add).then_inc(c_ready, 1)

            def sample_conv(j):
                out = C[:, j, SEQ:T]
                dve.wait_ge(win_ready, j + 1)
                seq(dve.tensor_reduce(out.rearrange("p (b t) -> p b t", b=NB), win[:], AX.X, ALU.add))
                dve.tensor_scalar(out, out, v("b_dw", j), None, ALU.add).then_inc(cs_ready, 1)

            taps = [(j, w) for j in range(DVE_CONV) for w in range(CW)]
            dve.wait_ge(in_state, 16)
            dve.wait_ge(in_dw, 16)
            for j in range(KT_D):
                lo_to(j + RING)
                dve.wait_ge(sig_ready, j + 1)
                dve.scalar_tensor_tensor(out=Us[:, j, :, CW - 1:CW - 1 + DS],
                                         in0=bank[2 * (j % 2)][:, SEQ:T].rearrange("p (b t) -> p b t", b=NB),
                                         scalar=v("b_a", j),
                                         in1=gate_s[:, j % 2, SEQ:T].rearrange("p (b t) -> p b t", b=NB),
                                         op0=ALU.add, op1=ALU.mult)
                dve.scalar_tensor_tensor(out=Up[:, j, CW - 1:CW - 1 + SEQ], in0=bank[2 * (j % 2)][:, 0:SEQ],
                                         scalar=v("b_a", j), in1=gate_s[:, j % 2, 0:SEQ],
                                         op0=ALU.add, op1=ALU.mult).then_inc(u_ready, 1)
                if j == 1:
                    dve.wait_ge(rel_sum, 1)
                    dve.tensor_copy(rb[:], bank[5][0:NH, 0:RLEN]).then_inc(rb_ready, 1)
                if j >= 1:
                    sample_conv(j - 1)
                for t in taps[TAPS_BETWEEN * j:TAPS_BETWEEN * j + TAPS_BETWEEN]:
                    tap(*t)
            sample_conv(KT_D - 1)
            for t in taps[TAPS_BETWEEN * KT_D:]:
                tap(*t)
            lo_to(U_PW2 + RING)
            dve.wait_ge(mean_ready, 1)
            dve.wait_ge(c_ready, DVE_CONV)
            dve.wait_ge(cs_ready, KT_D)
            dve.wait_ge(cp_ready, PE_CONV)
            for k in range(KT_D):
                dve.tensor_tensor(C[:, k, :], C[:, k, :], MEAN[:, 0:T], ALU.subtract).then_inc(xc_ready, 1)
            inverse_root(1)
            dve.wait_ge(xc_ready, KT_D)
            for k in range(KT_D):
                dve.scalar_tensor_tensor(out=C[:, k, :], in0=C[:, k, :], scalar=v("g_ln", k), in1=rr[:],
                                         op0=ALU.mult, op1=ALU.mult).then_inc(ln_ready, 1)
            for k in range(1, KT_D, 2):
                h_lo_odd(1, k, H_hi, H_lo)
            for d in range(KT_D):
                dve.wait_ge(pw2_done, d + 1)
                dve.scalar_tensor_tensor(out=X[:, d, :], in0=bank[d % 4][:, 0:T], scalar=v("b_pw2", d),
                                         in1=X[:, d, :], op0=ALU.add, op1=ALU.add).then_inc(x_conv, 1)
                if d % 2 and d < KT_D - 1:
                    lo_to(U_PW2 + RING + d // 2 + 1)
            inverse_root(2)
            normed(2, "g_ffn", H_hi, H_lo)
            lo_to(U_GU[0] + RING)
            for half in range(2):
                for i in range(FH):
                    f = FH * half + i
                    lo_to(U_GU[half] + i + RING)
                    dve.wait_ge(silu_ready, f + 1)
                    if f >= RAW:
                        dve.wait_ge(a_ready, f - RAW + 1)
                    else:
                        dve.wait_ge(h_ready[f % 2], h_count(2, KT_D - RAW + f))
                    dve.tensor_tensor(raw[:, f % RAW, :], gate_f[:, f % 2, :], bank[2 * (f % 2) + 1][:, 0:T],
                                      ALU.mult).then_inc(a_raw, 1)
                for d in range(KT_D):
                    lo_to(U_DOWN[half] + min(DOWN_UNITS, FH * d // BPU) + RING)
                    dve.wait_ge(down_done, KT_D * half + d + 1)
                    dve.tensor_tensor(X[:, d, :], bank[4 + d % 2][:, 0:T], X[:, d, :], ALU.add).then_inc(x_ffn, 1)
                if half == 0:
                    lo_to(U_GU[1] + 3)
            inverse_root(3)
            normed(3, "g_kv", H_hi, H_lo)
            normed(4, "g_attn", G_hi, G_lo)
            lo_to(U_K + RING)

            def head_norm(i, out, gain):
                src = bank[i] if i < 2 else bank[(i - 2) % 4]
                dve.wait_ge(kq_sd, i + 1)
                seq(dve.reciprocal(raw[:, i % 2, :], sd[:]))
                dve.scalar_tensor_tensor(out=out, in0=src[:, 0:T], scalar=gain, in1=raw[:, i % 2, :],
                                         op0=ALU.mult, op1=ALU.mult).then_inc(kq_ready, 1)

            dve.wait_ge(h_ready[0], 5 * KT_D // 2)
            dve.wait_ge(h_ready[1], 5 * KT_D // 2)
            head_norm(0, K[:, 0, :], v("g_k"))
            head_norm(1, K[:, 1, :], v("g_k"))
            dve.wait_ge(v_done, 1)
            dve.tensor_copy(V[:, 0:2, :], bank[2][:, :].rearrange("p (a n) -> p a n", a=2))
            dve.tensor_copy(V[0:NS, 2, :], bank[3][0:NS, 0:256]).then_inc(v_ready, 1)
            lo_to(U_V + RING)
            dve.wait_ge(in_kc, 16)
            dve.wait_ge(kq_ready, 2)
            dve.tensor_copy(KC[:, :, :, WIN:WIN + DS],
                            K[:, :, SEQ:T].rearrange("p n (b t) -> p n b t", b=NB)).then_inc(kc_ready, 1)
            for t in range(KT_D):
                lo_to(U_Q + t // 2 + RING)
                head_norm(2 + t, Q[:, t, :], g_q8[:])

            def soft_args(s):
                sm = small[:, s % 2, :]
                dve.wait_ge(sc_done, s + 1)
                if STEPS[s] is None:
                    dve.wait_ge(in_bias_s, 64)
                    own = c("own_new").rearrange("p (a b t) -> p a b t", a=4, b=NB)
                    seq(dve.tensor_tensor(bias_o[:], own, bias_n.unsqueeze(1).unsqueeze(1).to_broadcast([P, 4, NB, DS]), ALU.add))
                    for h in range(2):
                        src = bank[2 * (s % 2) + h][:, 0:2 * (WIN + NS)].rearrange("p (a s) -> p a s", a=2)
                        dve.tensor_tensor(SS[:, 2 * h:2 * h + 2, 0:WIN], src[:, :, 0:WIN],
                                          bias_c.unsqueeze(1).to_broadcast([P, 2, WIN]), ALU.add)
                        last = dve.tensor_tensor(SS[:, 2 * h:2 * h + 2, WIN:WIN + NS], src[:, :, WIN:WIN + NS],
                                                 bias_o[:, 2 * h:2 * h + 2].rearrange("p a b t -> p a (b t)"), ALU.add)
                    last.then_inc(s_ready, 1)
                    dve.wait_ge(s_ready, s + 1)
                    seq(dve.tensor_reduce(sm[:, 0:4], SS[:], AX.X, ALU.max))
                    seq(dve.tensor_scalar(sm[:, 0:4], sm[:, 0:4], v("sink_row"), None, ALU.max))
                    dve.tensor_scalar(sm[:, 4:8], sm[:, 0:4], -1.0, None, ALU.mult).then_inc(nm_ready, 1)
                    dve.wait_ge(nm_ready, s + 1)
                    dve.tensor_scalar(sm[:, 12:16], sm[:, 4:8], v("sink_row"), None, ALU.add).then_inc(es_arg, 1)
                    return
                n, b = STEPS[s]
                w = (b + 1) * P
                dve.wait_ge(in_bias[n % 2], 16 * (n // 2 + 1))
                if s >= 2:
                    dve.wait_ge(pT_done, TURNS[s - 1])
                for h in range(b + 1):
                    gs = GR // (b + 1)
                    a = 512 * h
                    last = dve.tensor_tensor(S[:, s % 2, a:a + 512].rearrange("p (g s) -> p g s", g=gs),
                                             bank[2 * (s % 2) + h][:, :].rearrange("p (g s) -> p g s", g=gs),
                                             bias[:, n % 2, gs * h:gs * h + gs, 2 * P - w:2 * P], ALU.add)
                last.then_inc(s_ready, 1)
                dve.wait_ge(s_ready, s + 1)
                seq(dve.tensor_reduce(sm[:, 0:4], S[:, s % 2, 0:GR * w].rearrange("p (g s) -> p g s", g=GR),
                                      AX.X, ALU.max))
                seq(dve.tensor_tensor(sm[:, 0:4], sm[:, 0:4], v("sinks", GR * n, GR), ALU.max))
                dve.tensor_scalar(sm[:, 4:8], sm[:, 0:4], -1.0, None, ALU.mult).then_inc(nm_ready, 1)
                dve.tensor_tensor(sm[:, 12:16], v("sinks", GR * n, GR), sm[:, 0:4],
                                  ALU.subtract).then_inc(es_arg, 1)

            def normalise(s):
                sm = small[:, s % 2, :]
                dve.wait_ge(p_ready, s + 1)
                seq(dve.tensor_tensor(sm[:, 20:24], sm[:, 8:12], sm[:, 16:20], ALU.add))
                seq(dve.reciprocal(sm[:, 20:24], sm[:, 20:24]))
                for g in range(GR):
                    if STEPS[s] is None:
                        part = SS[:, g, :]
                    else:
                        w = (STEPS[s][1] + 1) * P
                        part = S[:, s % 2, w * g:w * g + w]
                    last = dve.tensor_scalar(part, part, sm[:, 20 + g:21 + g], None, ALU.mult)
                last.then_inc(pn_ready, 1)

            def o_lo(s):
                dve.wait_ge(o_hi_ready, OUT_STEPS.index(s) + 1)
                if STEPS[s] is None:
                    for ng in range(2):
                        for i in range(2):
                            rows = slice(HD * i, HD * i + HD)
                            last = dve.tensor_tensor(sample_rows(H_lo, rows, ng), sample_out(rows, ng, i),
                                                     sample_rows(H_hi, rows, ng).bitcast(F32), ALU.subtract)
                else:
                    n, b = STEPS[s]
                    ng = n // 2
                    last = dve.tensor_tensor(H_lo[:, GR * ng:GR * ng + GR, P * b:P * b + P],
                                             bank[6 + b][:, :].rearrange("p (g q) -> p g q", g=GR),
                                             H_hi[:, GR * ng:GR * ng + GR, P * b:P * b + P].bitcast(F32),
                                             ALU.subtract)
                last.then_inc(o_ready, 1)

            soft_args(0)
            dve.wait_ge(kq_ready, 2 + KT_D)
            seq(dve.memset(QZ, 0.0))
            for ng in range(2):
                for i in range(2):
                    rows = slice(HD * i, HD * i + HD)
                    a = (2 * ng + i) * GR * DS
                    last = dve.tensor_copy(QZ[rows, ng, :, a:a + GR * DS].rearrange("p b (g t) -> p g b t", g=GR),
                                           sample_rows(Q, rows, ng))
            last.then_inc(qz_ready, 1)
            for s in range(len(STEPS)):
                if s + 1 < len(STEPS):
                    soft_args(s + 1)
                normalise(s)
                if s == 0:
                    lo_to(DENSE)
                if s - 1 in OUT_STEPS:
                    o_lo(s - 1)
            o_lo(len(STEPS) - 1)
            def expert_lo(trip, ch, j):
                n, slot = DENSE + 2 * ch + j, (DENSE + 3 * ch + j) % LAND
                dve.wait_ge(hi_done, trip * (2 * NCH) + n + 1)
                dve.tensor_tensor(w_lo[n % RING][:], land[slot][:], w_hi[n % RING][:].bitcast(F32),
                                  ALU.subtract).then_inc(split, 1)

            for d in range(KT_D):
                dve.wait_ge(wo_done, d + 1)
                dve.tensor_tensor(X[:, d, :], bank[d % 4][:, 0:T], X[:, d, :], ALU.add).then_inc(x_attn, 1)
                if d % 2 and d < KT_D - 1:
                    expert_lo(0, *FIRST_UNITS[d // 2])
            inverse_root(4)
            dve.wait_ge(kv_stored, 80)
            for k in range(KT_D):
                dve.scalar_tensor_tensor(out=Hm[:, k, :], in0=X[:, k, :], scalar=v("g_moe", k), in1=rr[:],
                                         op0=ALU.mult, op1=ALU.mult).then_inc(hm_ready, 1)
            expert_lo(0, *FIRST_UNITS[3])
            LG, SEL, EX, DIFF, TMP, COMB = (lg[:, i] for i in range(6))
            seq(dve.memset(lg[:], 0.0))
            dve.wait_ge(lg_done, 1)
            dve.tensor_copy(LG[:, 0:2, :], bank[0][:, 0:2 * NE].rearrange("p (i e) -> p i e", i=2))
            seq(dve.tensor_copy(LG[0:NS, 2, :], bank[0][0:NS, 2 * NE:3 * NE]))
            seq(dve.tensor_reduce(top[:, 0:3], LG, AX.X, ALU.max))
            dve.tensor_tensor(DIFF, LG, top[:, 0:3].unsqueeze(2).to_broadcast([P, 3, NE]),
                              ALU.subtract).then_inc(lg_ready, 1)
            other = LG.unsqueeze(2).to_broadcast([P, 3, NE, NE])
            mine = LG.unsqueeze(3).to_broadcast([P, 3, NE, NE])
            tie = c("tie").rearrange("p (e f) -> p e f", e=NE).unsqueeze(1).to_broadcast([P, 3, NE, NE])
            dve.tensor_tensor(cmp_[:, 0], other, mine, ALU.is_gt)
            seq(dve.tensor_tensor(cmp_[:, 1], other, mine, ALU.is_equal))
            seq(dve.tensor_tensor(cmp_[:, 1], cmp_[:, 1], tie, ALU.mult))
            seq(dve.tensor_tensor(cmp_[:, 0], cmp_[:, 0], cmp_[:, 1], ALU.add))
            seq(dve.tensor_reduce(TMP, cmp_[:, 0], AX.X, ALU.add))
            dve.tensor_scalar(SEL, TMP, TOP_K - 0.5, None, ALU.is_lt).then_inc(sel_ready, 1)
            dve.wait_ge(sel_ready, 1)
            dve.wait_ge(ex_ready, 1)
            seq(dve.tensor_tensor(EX, EX, SEL, ALU.mult))
            seq(dve.tensor_reduce(top[:, 4:7], EX, AX.X, ALU.add))
            seq(dve.reciprocal(top[:, 4:7], top[:, 4:7]))
            seq(dve.tensor_tensor(COMB, EX, top[:, 4:7].unsqueeze(2).to_broadcast([P, 3, NE]), ALU.mult))
            seq(dve.tensor_scalar(TMP, SEL, -NOT_HERE, NOT_HERE, ALU.mult, ALU.add))
            dve.wait_ge(pos_done, 1)
            dve.tensor_tensor(TMP[:, 0:2, :], TMP[:, 0:2, :], bank[0][:, 32:32 + 2 * NE].rearrange("p (i e) -> p i e", i=2), ALU.add)
            seq(dve.tensor_tensor(TMP[0:NS, 2, :], TMP[0:NS, 2, :], bank[0][0:NS, 32 + 2 * NE:32 + 3 * NE], ALU.add))
            for p in range(PASSES):
                dve.tensor_copy(gate_of[:, :, NE * p:NE * p + NE], COMB)
                dve.tensor_scalar(slot_of[:, :, NE * p:NE * p + NE], TMP, -float(SLOTS * p), None, ALU.add)
            seq(dve.tensor_reduce(top[:, 8:9], bank[0][:, 64:64 + NE], AX.X, ALU.max))
            seq(dve.tensor_scalar(top[:, 9:10], top[:, 8:9], SLOTS + 0.5, 1.0, ALU.is_gt, ALU.add))
            seq(dve.tensor_scalar(top[:, 10:11], top[:, 8:9], 2 * SLOTS + 0.5, None, ALU.is_gt))
            seq(dve.tensor_tensor(top[:, 11:12], top[:, 9:10], top[:, 10:11], ALU.add))
            seq(dve.tensor_scalar(top[:, 12:13], top[:, 11:12], float(NE), None, ALU.mult))
            dve.tensor_copy(trips[0:1, 0:2], top[0:1, 11:13]).then_inc(route_ready, 1)
            for m in range(6):
                i, h = divmod(m, 2)
                nt = TT[i][1]
                dve.wait_ge(htok_done, m + 1)
                dve.tensor_copy(H_tok[0:nt, i, 512 * h:512 * h + 512], bank[1 + m][0:nt, :]).then_inc(htok_ready, 1)
            dve.wait_ge(route_ready, 1)
            n_trips = dve.value_load(trips[0:1, 1:2], min_val=NE, max_val=PASSES * NE)

            def place(t):
                for i, (t0, nt) in enumerate(TT):
                    dve.tensor_scalar(P01[0:nt, i, :], c("iota")[0:nt, :], slot_of[0:nt, i, bass.ds(t, 1)], None,
                                      ALU.is_equal)
                    last = dve.tensor_scalar(PG[0:nt, i, :], c("iota")[0:nt, :], slot_of[0:nt, i, bass.ds(t, 1)],
                                             gate_of[0:nt, i, bass.ds(t, 1)], ALU.is_equal, ALU.mult)
                last.then_inc(P_ready, 1)

            def xe_rest(first, h):
                dve.wait_ge(xe_hi_ready, first + h + 1)
                dve.tensor_tensor(xe_lo[:, 512 * h:512 * h + 512], bank[4 + h][:, :],
                                  xe_hi[:, 512 * h:512 * h + 512].bitcast(F32), ALU.subtract).then_inc(xe_ready, 1)

            def add_back(trip, k):
                dve.wait_ge(y_done, trip * KT_D + k + 1)
                dve.tensor_tensor(X[:, k, :], bank[7][:, 0:T], X[:, k, :], ALU.add).then_inc(y_added, 1)

            place(0)
            dve.memset(oe[:], 0.0).then_inc(oe_ready, 2)
            dve.memset(PT[:], 0.0).then_inc(PT_ready, 1)
            dve.wait_ge(htok_ready, 6)
            xe_rest(0, 0)
            xe_rest(0, 1)
            with dve.Fori(0, n_trips) as trip:
                for ch in range(NCH):
                    dve.wait_ge(esilu_ready, trip * NCH + ch + 1)
                    dve.tensor_tensor(he[:], silu_g[:], bank[ch % 2][:, CH:2 * CH], ALU.mult).then_inc(he_ready, 1)
                    if ch == GATES_AT + 1:
                        with dve.If(trip < n_trips - 1):
                            dve.wait_ge(PT_done, trip + 1)
                            place(trip + 1)
                    if ch == NCH - 1:
                        with dve.If(trip < n_trips - 1):
                            xe_rest((trip + 1) * 2, 0)
                    dve.wait_ge(heT_hi_ready, trip * NCH + ch + 1)
                    dve.tensor_tensor(heT_lo[:], bank[6][:, 0:CH], heT_hi[:].bitcast(F32),
                                      ALU.subtract).then_inc(heT_ready, 1)
                    if ch + 2 < NCH:
                        expert_lo(trip, ch + 2, 0)
                        expert_lo(trip, ch + 2, 1)
                    elif ch + 2 == NCH:
                        with dve.If(trip < n_trips - 1):
                            expert_lo(trip, ch + 2, 0)
                            expert_lo(trip, ch + 2, 1)
                    else:
                        with dve.If(trip < n_trips - 1):
                            xe_rest((trip + 1) * 2, 1)
                            expert_lo(trip, ch + 2, 0)
                            expert_lo(trip, ch + 2, 1)
                    if 1 <= ch <= KT_D:
                        add_back(trip, ch - 1)
                dve.wait_ge(d_used, trip * NCH + NCH + 2)
                dve.tensor_copy(oe[:, 512:1024], bank[3][:, :]).then_inc(oe_ready, 1)
            for k in range(KT_D):
                add_back(n_trips, k)

        @block.gpsimd
        def _(pool):
            def h_lo_even(a, hi, lo):
                for k in range(0, KT_D, 2):
                    m = KT_D * a + k
                    pool.wait_ge(h_hi_ready, m + 1)
                    pool.tensor_tensor(lo[:, k, :], raw[:, m % RAW, :], hi[:, k, :].bitcast(F32),
                                       ALU.subtract).then_inc(h_ready[0], 1)

            def diagonals(m):
                for g, taps in enumerate(GROUPS):
                    if m >= 1:
                        pool.wait_ge(diag_used, len(GROUPS) * (m - 1) + g + 1)
                    pool.tensor_tensor(diag[:, g, 0:len(taps), :],
                                       ident.unsqueeze(1).to_broadcast([P, len(taps), P]),
                                       w_dw[:, DVE_CONV + m, taps[0]:taps[-1] + 1].unsqueeze(2).to_broadcast(
                                           [P, len(taps), P]), ALU.mult).then_inc(diag_ready, 1)

            h_lo_even(0, H_hi, H_lo)
            pool.wait_ge(in_con, 16)
            pool.wait_ge(in_dw, 16)
            diagonals(0)
            for j in range(KT_D):
                pool.wait_ge(u_ready, j + 1)
                if j >= 1:
                    pool.wait_ge(cs_ready, j)
                first = Us[:, j, :, 0:1]
                windows = bass.AP(tensor=first.tensor, offset=first.offset,
                                  ap=[list(first.ap[0]), [DS + CW - 1, NB], [1, DS], [1, CW]])
                pool.tensor_tensor(win[:], windows, w_dw[:, j, :].unsqueeze(1).unsqueeze(1).to_broadcast(
                    [P, NB, DS, CW]), ALU.mult).then_inc(win_ready, 1)
                if j == 1:
                    pool.wait_ge(rb_ready, 1)
                    per_head = P * RLEN
                    pool.dma_start(bass.AP(tensor=io["rel_rows"].tensor, offset=0,
                                           ap=[[per_head, NH], [RLEN, P], [1, RLEN]]),
                                   rb[:].unsqueeze(1).to_broadcast([NH, P, RLEN])).then_inc(rb_stored, 16)
            pool.dma_start(io["conv_p"], Up[:, :, SEQ:SEQ + CW - 1]).then_inc(conv_stored, 16)
            pool.dma_start(io["conv_s"], Us[:]).then_inc(conv_stored, 16)
            for m in range(1, PE_CONV):
                diagonals(m)
            h_lo_even(1, H_hi, H_lo)
            h_lo_even(2, H_hi, H_lo)
            for f in range(FT):
                pool.wait_ge(a_hi_ready, f + 1)
                pool.tensor_tensor(A_lo[:, f % (FH + 1), :], raw[:, f % RAW, :],
                                   A_hi[:, f % (FH + 1), :].bitcast(F32), ALU.subtract).then_inc(a_ready, 1)
            h_lo_even(3, H_hi, H_lo)
            h_lo_even(4, G_hi, G_lo)
            pool.dma_start(io["v_s"][:, 0:WIN - DS, :].rearrange("b s n -> s b n"), io["vc"][DS:WIN, :, :]).then_inc(kv_stored, 16)
            pool.wait_ge(kc_ready, 1)
            pool.wait_ge(v_ready, 1)
            pool.dma_start(io["k_p"], K[:, :, P:2 * P]).then_inc(kv_stored, 16)
            pool.dma_start(io["k_s"], KC[:]).then_inc(kv_stored, 16)
            pool.dma_start(io["v_p"], V[:, 1, :]).then_inc(kv_stored, 16)
            pool.dma_start(bass.AP(tensor=io["v_s"].tensor, offset=(WIN - DS) * 256,
                                   ap=[[WIN * 256, NB], [256, DS], [1, 256]]), V[0:NS, 2, :]).then_inc(kv_stored, 16)

            def expert_lo(trip, ch):
                slot = (DENSE + 3 * ch + 2) % LAND
                pool.wait_ge(d_hi_done, trip * NCH + ch + 1)
                pool.tensor_tensor(d_lo[ch % 2][:], land[slot][:], d_hi[ch % 2][:].bitcast(F32),
                                   ALU.subtract).then_inc(d_split, 1)

            pool.sem_inc(d_split, 2)
            expert_lo(0, 0)
            pool.wait_ge(route_ready, 1)
            n_trips = pool.value_load(trips[0:1, 1:2], min_val=NE, max_val=PASSES * NE)
            with pool.Fori(0, n_trips) as trip:
                for ch in range(NCH):
                    if ch + 1 < NCH:
                        expert_lo(trip, ch + 1)
                with pool.If(trip < n_trips - 1):
                    expert_lo(trip, NCH)



def _t5_bucket(dist):
    n = np.maximum(dist, 0)
    exact = 16
    large = exact + (np.log(np.maximum(n, 1) / exact) / np.log(128 / exact) * (32 - exact)).astype(np.int32)
    return np.where(n < exact, n, np.minimum(large, 31)).astype(np.int32)


def _constants():
    con = np.zeros((P, NCON), np.float32)

    def put(name, a):
        lo, hi = CON[name]
        con[:, lo:hi] = a

    part = np.arange(P)
    put("ident", np.eye(P))
    put("mean_d", 1.0 / D)
    put("mean_head", (part[:, None] // HD == part[None, :] // HD) / HD)
    put("ones", 1.0)
    put("before", part[:, None] < part[None, :])
    put("iota", np.arange(SLOTS)[None, :])
    pair, seq_of_col = np.arange(4)[None, :, None], (np.arange(NS) // DS)[None, None, :]
    own = (2 * pair + (part // 64)[:, None, None]) == seq_of_col
    put("own_new", np.where(own, 0.0, MASKED).reshape(P, 4 * NS))
    put("tie", (np.arange(NE)[None, :] < np.arange(NE)[:, None]).reshape(1, -1))
    put("eps", EPS)
    dist = 255 - np.arange(RLEN)
    valid = (dist >= 0) & (dist < WIN)
    buckets = np.zeros((NREL, RLEN), np.float32)
    buckets[_t5_bucket(dist)[valid], np.arange(RLEN)[valid]] = 1.0
    buckets[NREL - 1] = np.where(valid, 0.0, MASKED)
    return con, buckets


def _blocks(w, order=None):
    r, n = w.shape
    return w.reshape(r // P, P, n // P, P).transpose(0, 2, 1, 3)


def _layout(i):
    f = {k: np.asarray(a) for k, a in i.items()}
    ch = lambda a: a.reshape(KT_D, P).T
    x = np.concatenate([f["x_prompt"].reshape(SEQ, D), f["x_sample"].reshape(NS, D)])
    x = x.reshape(T, KT_D, P).transpose(2, 1, 0)
    parts = {
        "g_conv": ch(f["g_conv_norm"]), "b_a": ch(f["b_pw1"][0, :D]), "b_g": ch(f["b_pw1"][0, D:]),
        "b_dw": ch(f["b_dw"]), "g_ln": ch(f["g_ln"]), "b_ln": ch(f["b_ln"]), "b_pw2": ch(f["b_pw2"]),
        "g_ffn": ch(f["g_ffn_norm"]), "g_kv": ch(f["g_kv_norm"]), "g_attn": ch(f["g_attn_norm"]),
        "g_moe": ch(f["g_moe_norm"]), "g_k": np.tile(f["g_k_norm"], 2)[:, None],
        "g_q": np.tile(f["g_q_norm"][0], 2)[:, None],
        "sink_row": np.tile(np.repeat(f["sinks"][0], DS), 2)[:, None],
        "sinks": np.tile(f["sinks"][0][None, :], (P, 1)),
        "router": f["w_router"][0].reshape(KT_D, P, NE).transpose(1, 0, 2).reshape(P, -1),
    }
    vec = np.concatenate([parts[n] for n in VEC], axis=1)
    heads = [NKV * 0 + GR * (2 * ng + i) + g for ng in range(2) for g in range(GR) for i in range(2)]
    perm = np.concatenate([np.arange(HD) + HD * h for h in heads])
    pw1, pw2 = _blocks(f["w_pw1"][0]), _blocks(f["w_pw2"][0])
    wg, wu, wdn = _blocks(f["w_gate"][0]), _blocks(f["w_up"][0]), _blocks(f["w_down"][0])
    wk = _blocks(f["w_kv"][:, :NKV * HD])
    wv = f["w_kv"][:, NKV * HD:]
    wq = _blocks(f["w_q"][0][:, perm])
    wo = _blocks(f["w_o"][0][perm, :])
    unit = lambda b: b.reshape(BPU, P, P).transpose(1, 0, 2).reshape(P, UNIT)
    units = [unit(np.concatenate([pw1[:, j], pw1[:, KT_D + j]])) for j in range(KT_D)]
    two = lambda w: [unit(np.concatenate([w[:, 2 * d], w[:, 2 * d + 1]])) for d in range(w.shape[1] // 2)]
    units += two(pw2)
    for half in range(2):
        fs = range(FH * half, FH * half + FH)
        units += [unit(np.concatenate([wg[:, t], wu[:, t]])) for t in fs]
        b = np.concatenate([wdn[FH * half:FH * half + FH, d] for d in range(KT_D)])
        b = np.concatenate([b, np.zeros((DOWN_UNITS * BPU - len(b), P, P), np.float32)])
        units += [unit(b[BPU * u:BPU * u + BPU]) for u in range(DOWN_UNITS)]
    units += two(wk)
    units += [wv.reshape(KT_D, P, 256).transpose(1, 0, 2).reshape(P, UNIT)]
    units += two(wq) + two(wo)
    w_expert = np.empty((NE, NCH, 3, P, UNIT), np.float32)
    gu = np.stack([f["w_e_gate"][0], f["w_e_up"][0]], axis=2)
    gu = gu.reshape(NE, 2, 4, P, 2, NCH, CH)
    w_expert[:, :, 0:2] = gu.transpose(0, 5, 1, 3, 2, 4, 6).reshape(NE, NCH, 2, P, UNIT)
    dn = f["w_e_down"][0].reshape(NE, NCH, 2, P, D)
    w_expert[:, :, 2] = dn.transpose(0, 1, 3, 2, 4).reshape(NE, NCH, P, UNIT)
    state = np.zeros((P, KT_D, NB, DS + CW - 1), np.float32)
    state[..., :CW - 1] = f["state_conv"][0].reshape(NB, CW - 1, KT_D, P).transpose(3, 2, 0, 1)
    kc = np.zeros((P, 2, NB, WIN + DS), np.float32)
    kc[..., :WIN] = f["cache_k_win"].reshape(NB, WIN, 2, P).transpose(3, 2, 0, 1)
    vc = f["cache_v_win"].reshape(NB, WIN, 256).transpose(1, 0, 2)
    con, buckets = _constants()
    relb = np.concatenate([f["rel_bias"], np.ones((1, NH), np.float32)])
    w_dw = f["w_dw"][0].reshape(CW, KT_D, P).transpose(2, 1, 0)
    return dict(x=x, vec=vec, w_dw=w_dw, con=con, relb=relb, buckets=buckets, state=state, kc=kc, vc=vc,
                w_dense=np.stack(units), w_expert=w_expert.reshape(NE, UPE, P, UNIT))


OUTS = {"y": [P, KT_D, T], "conv_p": [P, KT_D, CW - 1], "conv_s": [P, KT_D, NB, DS + CW - 1],
        "k_p": [P, 2, WIN], "k_s": [P, 2, NB, WIN + DS], "v_p": [WIN, 256], "v_s": [NB, WIN, 256]}


def kernel(**inputs):
    import concourse.bacc as bacc
    from concourse.bass_utils import run_bass_kernel_spmd

    nc = bacc.Bacc("TRN2", target_bir_lowering=False, num_devices=1)
    arrays = {f"in_{n}": np.ascontiguousarray(a) for n, a in _layout(inputs).items()}
    io = {n[3:]: nc.dram_tensor(n, list(a.shape), F32, kind="ExternalInput").ap() for n, a in arrays.items()}
    for n, shape in OUTS.items():
        io[n] = nc.dram_tensor(f"out_{n}", shape, F32, kind="ExternalOutput").ap()
    io["rel_rows"] = nc.dram_tensor("rel_rows", [NH * P * RLEN], F32, kind="Internal").ap()
    build(nc, io)
    r = run_bass_kernel_spmd(nc, [arrays], core_ids=[0]).results[0]
    o = {n: np.asarray(r[f"out_{n}"]) for n in OUTS}
    y = o["y"].transpose(2, 1, 0).reshape(T, D)
    chan = lambda a: np.moveaxis(a, (0, 1), (-1, -2)).reshape(*a.shape[2:], -1)
    k_p = chan(o["k_p"]).reshape(1, WIN, NKV, HD)
    k_s = chan(o["k_s"])[:, DS:].reshape(NB, WIN, NKV, HD)
    return (y[:SEQ].reshape(1, SEQ, D), y[SEQ:].reshape(NB, DS, D),
            chan(o["conv_p"]).reshape(1, 1, CW - 1, D), chan(o["conv_s"])[:, DS:].reshape(1, NB, CW - 1, D),
            k_p, k_s, o["v_p"].reshape(1, WIN, NKV, HD), o["v_s"].reshape(NB, WIN, NKV, HD))
```

```python
from contextlib import ExitStack

import numpy as np

import concourse.bass as bass
from concourse import mybir

F32 = mybir.dt.float32
F32R = mybir.dt.float32r
I32 = mybir.dt.int32
ALU = mybir.AluOpType
ACT = mybir.ActivationFunctionType
AX = mybir.AxisListType

P = 128
D = 1024
KT_D = D // P
SEQ, NB, DS = 256, 8, 4
NS = NB * DS
T = SEQ + NS
TT = [(0, 128), (128, 128), (256, NS)]
CW = 31
HD, NH, NKV, GR = 64, 16, 4, 4
WIN = 128
FF, FE, NE, TOP_K = 2816, 3584, 8, 2
FT = FF // P
FH = FT // 2
EPS = 1e-6
MASKED = -1e30
UNIT = 2048
BPU = UNIT // P
CH = 256
NCH = FE // CH
UPE = 3 * NCH
LAND, RING = 6, 4
RAW = 4
SLOTS = 128
PASSES = -(-T // SLOTS)
GATES_AT = KT_D + 2
NOT_HERE = 4096.0

PE_CONV = 3
POOL_CONV = 1
DVE_CONV = KT_D - PE_CONV
TAPS_BETWEEN = 6
TAPS = 8
GROUPS = [range(a, min(a + TAPS, CW)) for a in range(0, CW, TAPS)]

DOWN_UNITS = -(-KT_D * FH // BPU)
U_PW1 = 0
U_PW2 = U_PW1 + KT_D
U_GU = [U_PW2 + KT_D // 2, 0]
U_DOWN = [U_GU[0] + FH, 0]
U_GU[1] = U_DOWN[0] + DOWN_UNITS
U_DOWN[1] = U_GU[1] + FH
U_K = U_DOWN[1] + DOWN_UNITS
U_V = U_K + 1
U_Q = U_V + 1
U_O = U_Q + KT_D // 2
DENSE = U_O + KT_D // 2
DOWN_LAST = KT_D * FH - BPU * (DOWN_UNITS - 1)

VEC = {}
_at = 0
for _name, _n in (("g_conv", 8), ("b_a", 8), ("b_g", 8), ("b_dw", 8), ("g_ln", 8), ("b_ln", 8),
                  ("b_pw2", 8), ("g_ffn", 8), ("g_kv", 8), ("g_attn", 8), ("g_moe", 8),
                  ("g_k", 1), ("g_q", 1), ("sink_row", 1), ("sinks", NH), ("router", 8 * NE)):
    VEC[_name] = (_at, _at + _n)
    _at += _n
NVEC = _at
CON = {}
_at = 0
for _name, _n in (("ident", P), ("mean_d", P), ("mean_head", P), ("ones", P), ("before", P),
                  ("iota", SLOTS), ("own_new", 4 * NS), ("tie", NE * NE), ("eps", 1)):
    CON[_name] = (_at, _at + _n)
    _at += _n
NCON = _at
NREL = 33
RLEN = 384


def build(nc, io):
    with ExitStack() as ctx:
        def sb(name, shape, dt=F32, stack=ctx):
            return stack.enter_context(nc.sbuf_tensor(name, shape, dt))

        def sem(name):
            return ctx.enter_context(nc.semaphore(name))

        bank = [ctx.enter_context(nc.psum_tensor(f"bank{i}", [P, 512], F32)) for i in range(8)]
        STAT, MEAN = bank[7], bank[6]

        land = [sb(f"land{i}", [P, UNIT]) for i in range(LAND)]
        w_hi = [sb(f"w_hi{i}", [P, UNIT], F32R) for i in range(RING)]
        w_lo = [sb(f"w_lo{i}", [P, UNIT], F32R) for i in range(RING)]
        X = sb("X", [P, KT_D, T])
        vec = sb("vec", [P, NVEC])
        con = sb("con", [P, NCON])
        sq = sb("sq", [P, 2, T])
        stats = sb("stats", [P, 2, T])
        sd, rr = stats[:, 0, :], stats[:, 1, :]
        raw = sb("raw", [P, RAW, T])
        g_q8 = sb("g_q8", [P, 1])

        prod = raw[:, :, 0:SEQ]

        phases = [0]

        def phase(*tensors):
            phases[0] += 1
            with ExitStack() as stack:
                return [sb(f"{n}_{phases[0]}", s, dt, stack) for n, s, dt in tensors]

        conv_mem = phase(("H_hi", [P, KT_D, T], F32R), ("H_lo", [P, KT_D, T], F32R),
                         ("gate_s", [P, 2, T], F32), ("Up", [P, KT_D, SEQ + CW - 1], F32),
                         ("Us", [P, KT_D, NB, DS + CW - 1], F32), ("C", [P, KT_D, T], F32),
                         ("win", [P, NB, DS, CW], F32), ("odd", [P, SEQ], F32), ("w_dw", [P, KT_D, CW], F32),
                         ("diag", [P, len(GROUPS), TAPS, P], F32), ("relb", [NREL, NH], F32),
                         ("buckets", [NREL, RLEN], F32), ("rb", [NH, RLEN], F32))
        H_hi, H_lo, gate_s, Up, Us, C, win, odd, w_dw, diag, relb, buckets, rb = conv_mem
        _, _, gate_f, A_hi, A_lo = phase(
            ("H_hi", [P, KT_D, T], F32R), ("H_lo", [P, KT_D, T], F32R), ("gate_f", [P, 2, T], F32),
            ("A_hi", [P, FH + 1, T], F32R), ("A_lo", [P, FH + 1, T], F32R))
        attn = [("H_hi", [P, KT_D, T], F32R), ("H_lo", [P, KT_D, T], F32R),
                ("Q", [P, KT_D, T], F32), ("K", [P, 2, T], F32), ("V", [P, 3, 256], F32),
                ("KC", [P, 2, NB, WIN + DS], F32), ("VC", [WIN, NB, 256], F32),
                ("small", [P, 2, 32], F32)]
        _, _, Q, K, V, KC, VC, small, G_hi, G_lo = phase(
            *attn, ("G_hi", [P, KT_D, T], F32R), ("G_lo", [P, KT_D, T], F32R))
        bias, S, pT, SS, bias_o = phase(
            *attn, ("bias", [P, 2, GR, 2 * P], F32), ("S", [P, 2, GR * 2 * P], F32),
            ("pT", [P, 2, 512], F32), ("SS", [P, 4, WIN + NS], F32), ("bias_o", [P, 4, NB, DS], F32))[8:]
        raw_flat = raw[:].rearrange("p a t -> p (a t)")
        QZ = raw_flat[:, 0:16 * 64].rearrange("p (n b r) -> p n b r", n=2, b=NB)
        bias_c = raw_flat[:, 1024:1024 + WIN]
        bias_n = small[:, 0, 28:28 + DS]
        r_tok = small[:, 1, 28:31]
        pTc = sq[:].rearrange("p a t -> p (a t)")[:, 0:512]
        pTn = stats[:].rearrange("p a t -> p (a t)")[0:NS, 0:512]
        moe = [("d_hi0", [P, UNIT], F32R), ("d_hi1", [P, UNIT], F32R),
               ("d_lo0", [P, UNIT], F32R), ("d_lo1", [P, UNIT], F32R),
               ("H_tok", [P, 3, D], F32), ("pick", [P, 3, SLOTS], F32), ("PG", [P, 3, SLOTS], F32),
               ("PT", [SLOTS, T], F32), ("slot_of", [P, 3, PASSES * NE + 1], F32),
               ("gate_of", [P, 3, PASSES * NE + 1], F32), ("lg", [P, 6, 3, NE], F32), ("rt", [P, 3], F32),
               ("cmp", [P, 2, 3, NE, NE], F32), ("top", [P, 16], F32), ("trips", [1, 2], I32)]
        (d_hi0, d_hi1, d_lo0, d_lo1, H_tok, pick, PG, PT, slot_of, gate_of, lg, rt, cmp_, top, trips,
         xe_hi, xe_lo, silu_g, he, heT_hi, heT_lo, oe) = phase(
            *moe, ("xe_hi", [P, D], F32R), ("xe_lo", [P, D], F32R), ("silu_g", [P, CH], F32),
            ("he", [SLOTS, CH], F32), ("heT_hi", [P, CH], F32R), ("heT_lo", [P, CH], F32R),
            ("oe", [SLOTS, D], F32))
        Hm = phase(*moe, ("Hm", [P, KT_D, T], F32))[-1]
        d_hi, d_lo = [d_hi0, d_hi1], [d_lo0, d_lo1]

        def v(name, k=0, n=1):
            a = VEC[name][0] + k
            return vec[:, a:a + n]

        def c(name):
            return con[:, CON[name][0]:CON[name][1]]

        ident = c("ident")
        router = vec[:, VEC["router"][0]:VEC["router"][1]].rearrange("p (k e) -> p k e", k=KT_D)

        landed = [sem(f"landed{i}") for i in range(LAND)]
        hi_done = sem("hi_done")
        split = sem("split")
        used = sem("used")
        d_hi_done = sem("d_hi_done")
        d_split = sem("d_split")
        d_used = sem("d_used")
        in_vec, in_con, in_rel, in_state = (sem(n) for n in ("in_vec", "in_con", "in_rel", "in_state"))
        in_x = [sem(f"in_x{i}") for i in range(4)]
        sq_ready, sq_summed, sd_ready, rr_ready = (sem(n) for n in
                                                   ("sq_ready", "sq_summed", "sd_ready", "rr_ready"))
        raw_ready, h_hi_ready = sem("raw_ready"), sem("h_hi_ready")
        h_ready = [sem("h_ready_even"), sem("h_ready_odd")]
        dve_seq = sem("dve_seq")
        rel_sum, rb_ready, rb_stored = sem("rel_sum"), sem("rb_ready"), sem("rb_stored")
        sig_ready, u_ready = sem("sig_ready"), sem("u_ready")
        diag_ready, diag_used, cv_done, cp_ready = (sem(n) for n in ("diag_ready", "diag_used", "cv_done", "cp_ready"))
        in_dw, cs_ready, cg_ready = (sem(n) for n in ("in_dw", "cs_ready", "cg_ready"))
        tap_ready, tap_added = sem("tap_ready"), sem("tap_added")
        win_ready, c_ready, mean_ready, xc_ready, ln_ready = (
            sem(n) for n in ("win_ready", "c_ready", "mean_ready", "xc_ready", "ln_ready"))
        pw2_done, x_conv = sem("pw2_done"), sem("x_conv")
        g_scaled, silu_ready, a_raw, a_hi_ready, a_ready = (
            sem(n) for n in ("g_scaled", "silu_ready", "a_raw", "a_hi_ready", "a_ready"))
        down_done, x_ffn = sem("down_done"), sem("x_ffn")
        kq_done, kq_sq, kq_ms, kq_sd, kq_ready = (
            sem(n) for n in ("kq_done", "kq_sq", "kq_ms", "kq_sd", "kq_ready"))
        v_done, v_ready, in_kc, in_vc = sem("v_done"), sem("v_ready"), sem("in_kc"), sem("in_vc")
        in_bias = [sem("in_bias0"), sem("in_bias1")]
        sc_done, s_ready, nm_ready, es_arg, p_ready, pn_ready = (
            sem(n) for n in ("sc_done", "s_ready", "nm_ready", "es_arg", "p_ready", "pn_ready"))
        pT_done, pT_ready, pv_done, o_hi_ready, o_ready = (
            sem(n) for n in ("pT_done", "pT_ready", "pv_done", "o_hi_ready", "o_ready"))
        kq_copied = sem("kq_copied")
        qz_zero, kq_scaled, rt_done, rt_ready = (sem(n) for n in ("qz_zero", "kq_scaled", "rt_done", "rt_ready"))
        qz_ready, kc_ready, in_bias_s = sem("qz_ready"), sem("kc_ready"), sem("in_bias_s")
        wo_done, x_attn = sem("wo_done"), sem("x_attn")
        hm_ready, lg_done, lg_ready, htok_done, htok_ready, ex_ready, sel_ready, pos_done, route_ready = (
            sem(n) for n in ("hm_ready", "lg_done", "lg_ready", "htok_done", "htok_ready", "ex_ready",
                             "sel_ready", "pos_done", "route_ready"))
        PG_ready = sem("PG_ready")
        P_ready, gathered, xe_hi_ready, xe_ready, PT_done, PT_ready = (
            sem(n) for n in ("P_ready", "gathered", "xe_hi_ready", "xe_ready", "PT_done", "PT_ready"))
        esilu_ready, he_ready, heT_done, heT_hi_ready, heT_ready = (
            sem(n) for n in ("esilu_ready", "he_ready", "heT_done", "heT_hi_ready", "heT_ready"))
        oe_ready, y_done, y_added = (
            sem(n) for n in ("oe_ready", "y_done", "y_added"))
        stored, conv_stored, kv_stored = sem("stored"), sem("conv_stored"), sem("kv_stored")

        STEPS = [(0, 0), (0, 1), (1, 0), (1, 1), None, (2, 0), (2, 1), (3, 0), (3, 1)]
        TURNS = [0]
        for _step in STEPS:
            TURNS.append(TURNS[-1] + (2 if _step is None else _step[1] + 1))
        owner = [i for i in range(len(STEPS)) for _ in range(TURNS[i + 1] - TURNS[i])]
        OUT_STEPS = [i for i, _step in enumerate(STEPS) if _step is None or _step[0] % 2 == 1]

        FIRST_UNITS = [(0, 0), (0, 1), (1, 0), (1, 1)]

        def sample_out(rows, ng, i):
            return bank[6][rows, 256 * ng:256 * ng + 256].rearrange("p (b i g t) -> p i g b t", b=NB, i=2, g=GR)[:, i]

        def sample_rows(dst, rows, ng):
            return dst[rows, GR * ng:GR * ng + GR, SEQ:T].rearrange("p g (b t) -> p g b t", b=NB)

        def h_number(a, k):
            return KT_D * a + k if a < 3 else 3 * KT_D + 2 * k + (a - 3)

        def toeplitz(head, n_heads, rows, first, cols):
            per_head = P * RLEN
            return bass.AP(tensor=io["rel_rows"].tensor, offset=head * per_head + first,
                           ap=[[RLEN - 1, rows], [per_head, n_heads], [1, cols]])

        block = ctx.enter_context(nc.Block())

        @block.sync
        def _(sp):
            for i in range(4):
                sp.dma_start(X[:, 2 * i:2 * i + 2, :], io["x"][:, 2 * i:2 * i + 2, :]).then_inc(in_x[i], 16)
            for n in range(DENSE):
                if n >= LAND:
                    sp.wait_ge(split, n - LAND + 1)
                cols = UNIT
                if n in (U_DOWN[0] + DOWN_UNITS - 1, U_DOWN[1] + DOWN_UNITS - 1):
                    cols = DOWN_LAST * P
                sp.dma_start(land[n % LAND][:, 0:cols], io["w_dense"][n, :, 0:cols]).then_inc(landed[n % LAND], 16)

            def expert_pass(first_trip):
                with sp.Fori(0, NE) as e:
                    trip = sp.snap(first_trip + e)
                    for u in range(UPE):
                        ch, j = divmod(u, 3)
                        if u < LAND:
                            sp.wait_ge(split, DENSE - LAND + 1 + u)
                        if j < 2:
                            sp.wait_ge(split, trip * (2 * NCH) + (DENSE + 2 * (ch - 2) + j + 1))
                        else:
                            sp.wait_ge(d_split, trip * NCH + (ch + 1))
                        slot = (DENSE + u) % LAND
                        sp.dma_start(land[slot][:], io["w_expert"][bass.ds(e, 1), u, :, :].rearrange(
                            "a p n -> (a p) n")).then_inc(landed[slot], 16)

            expert_pass(0)
            sp.wait_ge(route_ready, 1)
            passes = sp.value_load(trips[0:1, 0:1], min_val=1, max_val=PASSES)
            with sp.If(passes > 1):
                with sp.Fori(1, passes) as p:
                    expert_pass(p * NE)
            n_trips = sp.value_load(trips[0:1, 1:2], min_val=NE, max_val=PASSES * NE)
            for half in range(2):
                sp.wait_ge(y_added, n_trips * KT_D + 4 * (half + 1))
                sp.dma_start(io["y"][:, 4 * half:4 * half + 4, :], X[:, 4 * half:4 * half + 4, :]).then_inc(stored, 16)
            sp.wait_ge(stored, 32)
            sp.wait_ge(conv_stored, 32)
            sp.wait_ge(kv_stored, 80)

        @block.tensor
        def _(pe):
            def mm3(out, w, x, start, stop):
                pe.matmul(out, w[0], x[0], start=start, stop=False)
                pe.matmul(out, w[0], x[1], start=False, stop=False)
                return pe.matmul(out, w[1], x[0], start=False, stop=stop)

            def wblock(n, i):
                a, b = i * P, (i + 1) * P
                return w_hi[n % RING][:, a:b], w_lo[n % RING][:, a:b]

            def H(k, a=0, b=T):
                return H_hi[:, k, a:b], H_lo[:, k, a:b]

            def G(k):
                return G_hi[:, k, :], G_lo[:, k, :]

            def wait_h(a, k):
                m = h_number(a, k)
                pe.wait_ge(h_ready[m % 2], m // 2 + 1)

            def mean_part(q, k):
                pe.wait_ge(sq_ready, KT_D * q + k + 1)
                pe.matmul(STAT[:, 0:T], c("mean_d"), sq[:, k % 2, :], start=(k == 0),
                          stop=(k == KT_D - 1)).then_inc(sq_summed, 1)

            pe.wait_ge(in_con, 16)
            for k in range(KT_D):
                mean_part(0, k)
            for j in range(KT_D):
                pe.wait_ge(split, U_PW1 + j + 1)
                if j >= 2:
                    pe.wait_ge(u_ready, j - 1)
                for half in range(2):
                    out = bank[2 * (j % 2) + half][:, 0:T]
                    for k in range(KT_D):
                        if j == 0 and half == 0:
                            wait_h(0, k)
                        last = mm3(out, wblock(U_PW1 + j, KT_D * half + k), H(k), k == 0, k == KT_D - 1)
                last.then_inc(used, 1)
                if j == 0:
                    pe.wait_ge(in_rel, 32)
                    pe.matmul(bank[5][0:NH, 0:RLEN], relb[:, :], buckets[:, :], start=True, stop=True).then_inc(rel_sum, 1)
            for m, j in enumerate(range(DVE_CONV, KT_D)):
                if m == 0:
                    pe.wait_ge(rb_ready, 1)
                if m >= 2:
                    pe.wait_ge(cp_ready, m - 1)
                pe.wait_ge(u_ready, j + 1)
                for g, taps in enumerate(GROUPS):
                    pe.wait_ge(diag_ready, len(GROUPS) * m + g + 1)
                    for w in taps:
                        last = pe.matmul(bank[4 + m % 2][:, 0:SEQ], diag[:, g, w - taps[0], :], Up[:, j, w:w + SEQ],
                                         start=(w == 0), stop=(w == CW - 1))
                    last.then_inc(diag_used, 1)
                pe.wait_ge(diag_used, len(GROUPS) * (m + 1))
                pe.sem_inc(cv_done, 1)
            pe.wait_ge(cs_ready, KT_D)
            by_end = [*range(DVE_CONV - 1), *range(DVE_CONV, KT_D), DVE_CONV - 1]
            for k in by_end:
                if k < POOL_CONV:
                    pe.wait_ge(cg_ready, k + 1)
                elif k < DVE_CONV:
                    pe.wait_ge(c_ready, k - POOL_CONV + 1)
                else:
                    pe.wait_ge(cp_ready, k - DVE_CONV + 1)
                last = pe.matmul(MEAN[:, 0:T], c("mean_d"), C[:, k, :], start=(k == by_end[0]), stop=(k == by_end[-1]))
            last.then_inc(mean_ready, 1)
            for k in range(KT_D):
                mean_part(1, k)
            for d in range(KT_D):
                n = U_PW2 + d // 2
                pe.wait_ge(split, n + 1)
                if d >= 4:
                    pe.wait_ge(x_conv, d - 3)
                for k in range(KT_D):
                    if d == 0:
                        wait_h(1, k)
                    last = mm3(bank[d % 4][:, 0:T], wblock(n, KT_D * (d % 2) + k), H(k), k == 0, k == KT_D - 1)
                last.then_inc(pw2_done, 1)
                if d % 2:
                    pe.wait_ge(pw2_done, d + 1)
                    pe.sem_inc(used, 1)
                if d >= 2:
                    mean_part(2, d - 2)
            mean_part(2, KT_D - 2)
            mean_part(2, KT_D - 1)
            for half in range(2):
                for i in range(FH):
                    f = FH * half + i
                    n = U_GU[half] + i
                    pe.wait_ge(split, n + 1)
                    if f >= 2:
                        pe.wait_ge(a_raw, f - 1)
                    for part in range(2):
                        out = bank[2 * (f % 2) + part][:, 0:T]
                        for k in range(KT_D):
                            if f == 0 and part == 0:
                                wait_h(2, k)
                            last = mm3(out, wblock(n, KT_D * part + k), G(k), k == 0, k == KT_D - 1)
                    last.then_inc(used, 1)
                for d in range(KT_D):
                    if KT_D * half + d >= 2:
                        pe.wait_ge(x_ffn, KT_D * half + d - 1)
                    for i in range(FH):
                        f = FH * half + i
                        unit, blk = divmod(FH * d + i, BPU)
                        n = U_DOWN[half] + unit
                        pe.wait_ge(split, n + 1)
                        pe.wait_ge(a_ready, f + 1)
                        a = f % (FH + 1)
                        last = mm3(bank[4 + d % 2][:, 0:T], wblock(n, blk), (A_hi[:, a, :], A_lo[:, a, :]),
                                   i == 0, i == FH - 1)
                        if blk == BPU - 1 and i < FH - 1:
                            last.then_inc(used, 1)
                    last.then_inc(down_done, 1)
                    if blk == BPU - 1 or d == KT_D - 1:
                        pe.wait_ge(down_done, KT_D * half + d + 1)
                        pe.sem_inc(used, 1)
                    if half == 1 and d >= 2:
                        mean_part(3, d - 2)
            mean_part(3, KT_D - 2)
            mean_part(3, KT_D - 1)
            pe.wait_ge(split, U_K + 1)
            for t in range(2):
                for k in range(KT_D):
                    if t == 0:
                        wait_h(3, k)
                    last = mm3(bank[t][:, 0:T], wblock(U_K, KT_D * t + k), H(k), k == 0, k == KT_D - 1)
                last.then_inc(kq_done, 1)
            pe.wait_ge(kq_done, 2)
            pe.sem_inc(used, 1)
            def head_mean(i):
                pe.wait_ge(kq_sq, i + 1)
                if i >= 2:
                    pe.wait_ge(kq_sd, i - 1)
                pe.matmul(bank[4 + i % 2][:, 0:T], c("mean_head"), sq[:, i % 2, :], start=True,
                          stop=True).then_inc(kq_ms, 1)

            pe.wait_ge(split, U_V + 1)
            for i, (t0, nt) in enumerate(TT):
                for k in range(KT_D):
                    a = k * 256
                    last = mm3(bank[2 + i // 2][0:nt, 256 * (i % 2):256 * (i % 2) + 256],
                               H(k, t0, t0 + nt), (w_hi[U_V % RING][:, a:a + 256], w_lo[U_V % RING][:, a:a + 256]),
                               k == 0, k == KT_D - 1)
                if i < 2:
                    head_mean(i)
            last.then_inc(v_done, 1)
            pe.wait_ge(v_done, 1)
            pe.sem_inc(used, 1)
            pe.wait_ge(rr_ready, 4)
            for i, (t0, nt) in enumerate(TT):
                last = pe.matmul(bank[6][0:nt, i:i + 1], rr[:, t0:t0 + nt], c("mean_head")[:, 0:1], start=True, stop=True)
            last.then_inc(rt_done, 1)

            for t in range(KT_D):
                n = U_Q + t // 2
                pe.wait_ge(split, n + 1)
                pe.wait_ge(kq_copied, t + 1 if t < 2 else max(2, t - 1))
                if t == 2:
                    pe.wait_ge(v_ready, 1)
                for k in range(KT_D):
                    if t == 0:
                        wait_h(4, k)
                    last = mm3(bank[t % 4][:, 0:T], wblock(n, KT_D * (t % 2) + k), G(k),
                               k == 0, k == KT_D - 1)
                last.then_inc(kq_done, 1)
                if t % 2:
                    pe.wait_ge(kq_done, 2 + t + 1)
                    pe.sem_inc(used, 1)
                if t >= 1:
                    head_mean(2 + t - 1)
            head_mean(2 + KT_D - 1)

            def scores(s):
                if s >= 2:
                    pe.wait_ge(s_ready, s - 1)
                if s == 4:
                    pe.wait_ge(kq_ready, 2 + KT_D)
                if STEPS[s] is None:
                    pe.wait_ge(qz_ready, 1)
                    for b in range(NB):
                        pair, half = divmod(b, 2)
                        at = (WIN + NS) * (pair % 2)
                        out = bank[2 * (s % 2) + pair // 2][64 * half:64 * half + 64, :]
                        for ng in range(2):
                            pe.matmul(out[:, at:at + WIN], QZ[:, ng, b, :], KC[:, ng, b, 0:WIN],
                                      start=(ng == 0), stop=(ng == 1))
                        for ng in range(2):
                            last = pe.matmul(out[:, at + WIN:at + WIN + NS], QZ[:, ng, b, :], K[:, ng, SEQ:T],
                                             start=(ng == 0), stop=(ng == 1))
                    last.then_inc(sc_done, 1)
                    return
                n, b = STEPS[s]
                ng, i = divmod(n, 2)
                rows = slice(HD * i, HD * i + HD)
                for g in range(GR):
                    q = Q[rows, GR * ng + g, P * b:P * b + P]
                    if b == 0:
                        last = pe.matmul(bank[2 * (s % 2)][:, P * g:P * g + P], q, K[rows, ng, 0:P],
                                         start=True, stop=True)
                    else:
                        last = pe.matmul(bank[2 * (s % 2) + g // 2][:, 2 * P * (g % 2):2 * P * (g % 2) + 2 * P],
                                         q, K[rows, ng, 0:2 * P], start=True, stop=True)
                last.then_inc(sc_done, 1)

            def attend(s):
                pe.wait_ge(pn_ready, s + 1)
                for m in range(TURNS[s], TURNS[s + 1]):
                    kb = m - TURNS[s]
                    if m >= 2:
                        pe.wait_ge(pT_ready, m - 1)
                    for g in range(GR):
                        out = bank[4 + m % 2][:, P * g:P * g + P]
                        if STEPS[s] is None:
                            src = SS[:, g, 0:WIN] if kb == 0 else SS[:, g, WIN:WIN + NS]
                            last = pe.transpose(out if kb == 0 else out[0:NS, :], src, ident)
                        else:
                            a = (g * (STEPS[s][1] + 1) + kb) * P
                            last = pe.transpose(out, S[:, s % 2, a:a + P], ident)
                    last.then_inc(pT_done, 1)
                if STEPS[s] is None:
                    pe.wait_ge(o_ready, OUT_STEPS.index(s))
                    pe.wait_ge(in_vc, 16)
                    pe.wait_ge(pT_ready, TURNS[s + 1])
                    for ng in range(2):
                        out = bank[6][:, 256 * ng:256 * ng + 256]
                        pe.matmul(out, V[0:NS, 2, P * ng:P * ng + P],
                                  pTn.rearrange("p (b n r) -> p b n r", b=NB, n=2)[:, :, ng, :], start=True, stop=False)
                        for b in range(NB):
                            a = 64 * b + 32 * ng
                            last = pe.matmul(out[:, 32 * b:32 * b + 32], VC[:, b, P * ng:P * ng + P],
                                             pTc[:, a:a + 32], start=False, stop=(b == NB - 1))
                    last.then_inc(pv_done, 1)
                    return
                n, b = STEPS[s]
                i = n % 2
                if n == 2:
                    pe.wait_ge(o_ready, 3 if b == 0 else 2)
                for kb in range(b + 1):
                    m = TURNS[s] + kb
                    pe.wait_ge(pT_ready, m + 1)
                    last = pe.matmul(bank[6 + b][HD * i:HD * i + HD, :], V[:, kb, HD * n:HD * n + HD],
                                     pT[:, m % 2, :], start=(kb == 0), stop=(kb == b))
                last.then_inc(pv_done, 1)

            pe.wait_ge(kq_copied, 2 + KT_D)
            pe.wait_ge(kq_ready, 2 + GR)
            scores(0)
            scores(1)
            for s in range(len(STEPS)):
                if s + 2 < len(STEPS):
                    scores(s + 2)
                attend(s)
            def route_sums(k):
                pe.wait_ge(sq_ready, KT_D * 4 + k + 1)
                pe.wait_ge(hm_ready, k + 1)
                if k == 0:
                    pe.wait_ge(PT_ready, 1)
                    pe.matmul(STAT[:, 0:32], ident, PT[:, 0:32], start=True, stop=False)
                for i, (t0, nt) in enumerate(TT):
                    last = pe.matmul(STAT[0:nt, i:i + 1], sq[:, k % 2, t0:t0 + nt], c("mean_d")[:, 0:1],
                                     start=False, stop=False)
                last.then_inc(sq_summed, 1)
                for i, (t0, nt) in enumerate(TT):
                    last = pe.matmul(STAT[0:nt, 8 + NE * i:8 + NE * i + NE], Hm[:, k, t0:t0 + nt], router[:, k, :],
                                     start=False, stop=False)
                if k == KT_D - 1:
                    pe.matmul(STAT[:, 0:32], ident, PT[:, 0:32], start=False, stop=True).then_inc(lg_done, 1)

            def to_tokens(k):
                if k >= 4:
                    pe.wait_ge(htok_ready, 3)
                for i, (t0, nt) in enumerate(TT):
                    last = pe.transpose(bank[4 + i][0:nt, P * (k % 4):P * (k % 4) + P], Hm[:, k, t0:t0 + nt], ident)
                if k % 4 == 3:
                    last.then_inc(htok_done, 1)

            pe.wait_ge(o_ready, len(OUT_STEPS))
            for d in range(KT_D):
                n = U_O + d // 2
                pe.wait_ge(split, n + 1)
                if d >= 4:
                    pe.wait_ge(x_attn, d - 3)
                for k in range(KT_D):
                    last = mm3(bank[d % 4][:, 0:T], wblock(n, KT_D * (d % 2) + k), H(k), k == 0, k == KT_D - 1)
                last.then_inc(wo_done, 1)
                if d % 2:
                    pe.wait_ge(wo_done, d + 1)
                    pe.sem_inc(used, 1)
                if d >= 2:
                    route_sums(d - 2)
                    to_tokens(d - 2)
            pe.wait_ge(kv_stored, 80)
            pe.sem_inc(d_used, 2)
            for k in (KT_D - 2, KT_D - 1):
                route_sums(k)
            for k in (KT_D - 2, KT_D - 1):
                to_tokens(k)
            sel = lg[:, 1]
            pe.wait_ge(sel_ready, 1)
            for i, (t0, nt) in enumerate(TT):
                for j in range(i + 1):
                    m = TT[j][1]
                    pe.matmul(STAT[0:nt, 32 + NE * i:32 + NE * i + NE], (c("before") if j == i else c("ones"))[0:m, 0:nt],
                              sel[0:m, j, :], start=(j == 0), stop=(j == i))
            for j in range(3):
                m = TT[j][1]
                last = pe.matmul(STAT[:, 64:64 + NE], c("ones")[0:m, :], sel[0:m, j, :], start=(j == 0), stop=(j == 2))
            last.then_inc(pos_done, 1)

            def gather(h):
                for k in range(4):
                    for j, (t0, nt) in enumerate(TT):
                        last = pe.matmul(bank[4 + h][:, P * k:P * k + P],
                                         H_tok[0:nt, j, (4 * h + k) * P:(4 * h + k + 1) * P],
                                         pick[0:nt, j, :], start=(j == 0), stop=(j == 2))
                last.then_inc(gathered, 1)

            def turn_gates():
                for j, (t0, nt) in enumerate(TT):
                    last = pe.transpose(bank[7][:, t0:t0 + nt], PG[0:nt, j, :], ident[0:nt, 0:nt])
                last.then_inc(PT_done, 1)

            pe.wait_ge(htok_ready, 6)
            pe.wait_ge(P_ready, 1)
            gather(0)
            gather(1)
            pe.wait_ge(route_ready, 1)
            n_trips = pe.value_load(trips[0:1, 1:2], min_val=NE, max_val=PASSES * NE)

            def back(trip, k, out=bank[7], banks=1):
                pe.wait_ge(oe_ready, trip * 2 + 2)
                pe.wait_ge(PT_ready, trip + 1)
                if k >= banks:
                    pe.wait_ge(y_added, trip * KT_D + (k - banks + 1))
                pe.matmul(out[:, 0:T], oe[:, P * k:P * k + P], PT[:, :], start=True, stop=True).then_inc(y_done, 1)

            with pe.Fori(0, n_trips) as trip:
                def gate_up(ch, h):
                    n = DENSE + 2 * ch + h
                    pe.wait_ge(split, trip * (2 * NCH) + n + 1)
                    for k in range(4):
                        kk = 4 * h + k
                        last = mm3(bank[ch % 2][:, :], (xe_hi[:, kk * P:kk * P + P], xe_lo[:, kk * P:kk * P + P]),
                                   (w_hi[n % RING][:, 512 * k:512 * k + 512], w_lo[n % RING][:, 512 * k:512 * k + 512]),
                                   kk == 0, kk == KT_D - 1)
                    last.then_inc(used, 1)

                def turn(ch):
                    pe.wait_ge(he_ready, trip * NCH + ch + 1)
                    for k in range(2):
                        last = pe.transpose(bank[6][:, P * k:P * k + P], he[:, P * k:P * k + P], ident)
                    last.then_inc(heT_done, 1)

                def down(ch):
                    pe.wait_ge(heT_ready, trip * NCH + ch + 1)
                    if ch == 0:
                        pe.wait_ge(oe_ready, trip * 2 + 2)
                    pe.wait_ge(d_split, trip * NCH + ch + 1 + 2)
                    for h in range(2):
                        for k in range(2):
                            a = D * k + 512 * h
                            last = mm3(bank[2 + h][:, :], (heT_hi[:, P * k:P * k + P], heT_lo[:, P * k:P * k + P]),
                                       (d_hi[ch % 2][:, a:a + 512], d_lo[ch % 2][:, a:a + 512]),
                                       ch == 0 and k == 0, ch == NCH - 1 and k == 1)
                    last.then_inc(d_used, 1)

                pe.wait_ge(xe_ready, trip * 2 + 1)
                gate_up(0, 0)
                pe.wait_ge(xe_ready, trip * 2 + 2)
                gate_up(0, 1)
                for ch in range(NCH):
                    if ch + 1 < NCH:
                        gate_up(ch + 1, 0)
                        turn(ch)
                        gate_up(ch + 1, 1)
                    else:
                        with pe.If(trip < n_trips - 1):
                            pe.wait_ge(P_ready, trip + 2)
                            gather(0)
                        turn(ch)
                        with pe.If(trip < n_trips - 1):
                            gather(1)
                    down(ch)
                    if 1 <= ch <= KT_D:
                        back(trip, ch - 1)
                    if ch == GATES_AT:
                        pe.wait_ge(PG_ready, trip + 1)
                        pe.wait_ge(y_added, trip * KT_D + KT_D)
                        turn_gates()
            for k in range(KT_D):
                back(n_trips, k, bank[4 + k % 4], 4)

        @block.scalar
        def _(act):
            act.dma_start(con[:], io["con"]).then_inc(in_con, 16)
            act.dma_start(vec[:], io["vec"]).then_inc(in_vec, 16)

            n_hi = 0

            def hi_to(m):
                nonlocal n_hi
                while n_hi < min(m, DENSE):
                    n = n_hi
                    act.wait_ge(landed[n % LAND], 16 * (n // LAND + 1))
                    if n >= RING:
                        act.wait_ge(used, n - RING + 1)
                    cols = DOWN_LAST * P if n in (U_DOWN[0] + DOWN_UNITS - 1, U_DOWN[1] + DOWN_UNITS - 1) else UNIT
                    act.copy(w_hi[n % RING][:, 0:cols], land[n % LAND][:, 0:cols]).then_inc(hi_done, 1)
                    n_hi += 1

            def square(q, src, k):
                if KT_D * q + k >= 2:
                    act.wait_ge(sq_summed, KT_D * q + k - 1)
                act.activation(sq[:, k % 2, :], src[:, k, :], ACT.Square).then_inc(sq_ready, 1)

            def root(q):
                act.wait_ge(sq_summed, KT_D * (q + 1))
                act.activation(sd[:], STAT[:, 0:T], ACT.Sqrt, bias=c("eps")).then_inc(sd_ready, 1)

            def h_hi(a, k, dst):
                m = h_number(a, k)
                act.wait_ge(raw_ready, m + 1)
                act.copy(dst[:, k, :], raw[:, m % RAW, :]).then_inc(h_hi_ready, 1)

            for k in range(KT_D):
                act.wait_ge(in_x[k // 2], 16)
                square(0, X, k)
            hi_to(1)
            act.wait_ge(in_con, 16)
            root(0)
            for k in range(KT_D):
                h_hi(0, k, H_hi)
            hi_to(RING)
            def tap(w):
                act.wait_ge(u_ready, 1)
                x, scale = Up[:, 0, w:w + SEQ], w_dw[:, 0, w:w + 1]
                if w == 0:
                    act.activation(C[:, 0, 0:SEQ], x, ACT.Identity, scale=scale, bias=v("b_dw", 0)).then_inc(tap_ready, 1)
                else:
                    if w > 4:
                        act.wait_ge(tap_added, w - 4)
                    act.activation(prod[:, w % 4, :], x, ACT.Identity, scale=scale).then_inc(tap_ready, 1)

            act.wait_ge(in_dw, 16)
            act.wait_ge(h_ready[0], KT_D // 2)
            act.wait_ge(h_ready[1], KT_D // 2)
            act.wait_ge(in_vec, 16)
            for j in range(KT_D):
                hi_to(j + RING)
                act.wait_ge(used, U_PW1 + j + 1)
                if j >= 2:
                    act.wait_ge(u_ready, j - 1)
                act.activation(gate_s[:, j % 2, :], bank[2 * (j % 2) + 1][:, 0:T], ACT.Sigmoid,
                               bias=v("b_g", j)).then_inc(sig_ready, 1)
                for w in range(4 * j, min(4 * j + 4, CW)):
                    tap(w)
            hi_to(U_PW2 + RING)
            for m, j in enumerate(range(DVE_CONV, KT_D)):
                act.wait_ge(cv_done, m + 1)
                act.activation(C[:, j, 0:SEQ], bank[4 + m % 2][:, 0:SEQ], ACT.Identity,
                               bias=v("b_dw", j)).then_inc(cp_ready, 1)
            act.wait_ge(cg_ready, POOL_CONV)
            for k in range(KT_D):
                act.wait_ge(xc_ready, k + 1)
                square(1, C, k)
            root(1)

            for k in range(KT_D):
                m = KT_D + k
                act.wait_ge(ln_ready, k + 1)
                act.wait_ge(h_ready[m % 2], m // 2 - 1)
                act.activation(raw[:, m % RAW, :], C[:, k, :], ACT.Silu, bias=v("b_ln", k)).then_inc(raw_ready, 1)
                if k >= 1:
                    h_hi(1, k - 1, H_hi)
            h_hi(1, KT_D - 1, H_hi)
            for k in range(KT_D):
                act.wait_ge(x_conv, k + 1)
                square(2, X, k)
                h_hi(2, k, G_hi)
                if k % 2 and k < KT_D - 1:
                    hi_to(U_PW2 + RING + k // 2 + 1)
            root(2)
            hi_to(U_GU[0] + RING)
            act.wait_ge(conv_stored, 32)
            for half in range(2):
                for i in range(FH):
                    f = FH * half + i
                    hi_to(U_GU[half] + i + RING)
                    act.wait_ge(g_scaled, f + 1)
                    act.activation(gate_f[:, f % 2, :], gate_f[:, f % 2, :], ACT.Silu).then_inc(silu_ready, 1)
                    act.wait_ge(a_raw, f + 1)
                    if half == 1:
                        act.wait_ge(down_done, KT_D)
                    act.copy(A_hi[:, f % (FH + 1), :], raw[:, f % RAW, :]).then_inc(a_hi_ready, 1)
                for d in range(KT_D):
                    hi_to(U_DOWN[half] + min(DOWN_UNITS, FH * d // BPU) + RING)
                    if half == 1:
                        act.wait_ge(x_ffn, KT_D + d + 1)
                        square(3, X, d)
                        h_hi(3, d, H_hi)
                        h_hi(4, d, G_hi)
                if half == 0:
                    hi_to(U_GU[1] + 3)
            root(3)
            act.dma_start(KC[:], io["kc"]).then_inc(in_kc, 16)
            act.dma_start(VC[:], io["vc"]).then_inc(in_vc, 16)
            hi_to(U_K + RING)

            def head_copy(i):
                act.wait_ge(kq_done, i + 1)
                act.copy(K[:, i, :] if i < 2 else Q[:, i - 2, :], bank[i if i < 2 else (i - 2) % 4][:, 0:T]).then_inc(kq_copied, 1)

            def head_square(i):
                src = K[:, i, :] if i < 2 else Q[:, i - 2, :]
                act.wait_ge(kq_scaled, i + 1)
                if i >= 2:
                    act.wait_ge(kq_ms, i - 1)
                act.activation(sq[:, i % 2, :], src, ACT.Square).then_inc(kq_sq, 1)

            def head_root(i):
                act.wait_ge(kq_ms, i + 1)
                if i >= 2:
                    act.wait_ge(kq_ready, i - 1)
                act.activation(raw[:, 2 + i % 2, :], bank[4 + i % 2][:, 0:T], ACT.Sqrt, bias=c("eps")).then_inc(kq_sd, 1)

            head_copy(0)
            head_copy(1)
            head_square(0)
            head_square(1)
            act.wait_ge(h_ready[0], 5 * KT_D // 2)
            act.wait_ge(h_ready[1], 5 * KT_D // 2)
            head_root(0)
            head_root(1)
            act.wait_ge(rt_done, 1)
            act.copy(r_tok[:, 0:2], bank[6][:, 0:2])
            act.copy(r_tok[0:NS, 2:3], bank[6][0:NS, 2:3]).then_inc(rt_ready, 1)
            act.wait_ge(rt_ready, 1)
            for i, (t0, nt) in enumerate(TT):
                last = act.activation(V[0:nt, i, :], bank[2 + i // 2][0:nt, 256 * (i % 2):256 * (i % 2) + 256],
                                      ACT.Identity, scale=r_tok[0:nt, i:i + 1])
            last.then_inc(v_ready, 1)
            hi_to(U_V + RING)
            for t in range(KT_D):
                head_copy(2 + t)
                if t >= 1:
                    head_root(2 + t - 1)
                head_square(2 + t)
                if t < KT_D - 2:
                    hi_to(U_Q + t // 2 + RING)
            act.wait_ge(rb_stored, 16)
            for n in range(2):
                act.dma_start(bias[:, n], toeplitz(GR * n, GR, P, P - 1, 2 * P)).then_inc(in_bias[n], 16)
            head_root(2 + KT_D - 1)

            def exps(s):
                sm = small[:, s % 2, :]
                act.wait_ge(nm_ready, s + 1)
                for g in range(GR):
                    if STEPS[s] is None:
                        part = SS[:, g, :]
                    else:
                        w = (STEPS[s][1] + 1) * P
                        part = S[:, s % 2, w * g:w * g + w]
                    act.activation(part, part, ACT.Exp, bias=sm[:, 4 + g:5 + g], accum_out=sm[:, 8 + g:9 + g])
                act.wait_ge(es_arg, s + 1)
                act.activation(sm[:, 16:20], sm[:, 12:16], ACT.Exp).then_inc(p_ready, 1)
                if STEPS[s] in ((0, 1), (1, 1)):
                    n = STEPS[s][0]
                    act.wait_ge(s_ready, s + 1)
                    act.dma_start(bias[:, n], toeplitz(GR * (n + 2), GR, P, P - 1, 2 * P)).then_inc(in_bias[n], 16)

            def o_hi(s):
                act.wait_ge(pv_done, s + 1)
                if STEPS[s] is None:
                    for ng in range(2):
                        for i in range(2):
                            rows = slice(HD * i, HD * i + HD)
                            last = act.copy(sample_rows(H_hi, rows, ng), sample_out(rows, ng, i))
                else:
                    n, b = STEPS[s]
                    ng = n // 2
                    last = act.copy(H_hi[:, GR * ng:GR * ng + GR, P * b:P * b + P],
                                    bank[6 + b][:, :].rearrange("p (g q) -> p g q", g=GR))
                last.then_inc(o_hi_ready, 1)

            exps(0)
            for s in range(len(STEPS)):
                if s + 1 < len(STEPS):
                    exps(s + 1)
                if s == 1:
                    hi_to(DENSE)
                if s - 1 in OUT_STEPS:
                    o_hi(s - 1)
                for m in range(TURNS[s], TURNS[s + 1]):
                    act.wait_ge(pT_done, m + 1)
                    if m >= 2:
                        act.wait_ge(pv_done, owner[m - 2] + 1)
                    if STEPS[s] is not None:
                        act.copy(pT[:, m % 2, :], bank[4 + m % 2][:, :]).then_inc(pT_ready, 1)
                    elif m == TURNS[s]:
                        act.copy(pTc, bank[4 + m % 2][:, :]).then_inc(pT_ready, 1)
                    else:
                        act.copy(pTn, bank[4 + m % 2][0:NS, :]).then_inc(pT_ready, 1)
                if s == 0:
                    act.wait_ge(kq_ready, 2 + KT_D)
                    per_head = P * RLEN
                    for two in range(2):
                        for dst, first, cols in ((bias_c, P - 1, WIN), (bias_n, 2 * P - 1, DS)):
                            act.dma_start(dst[64 * two:64 * two + 64, :],
                                          bass.AP(tensor=io["rel_rows"].tensor, offset=first,
                                                  ap=[[per_head, NH], [RLEN - 1, DS], [1, cols]])).then_inc(in_bias_s, 16)
            o_hi(len(STEPS) - 1)

            def expert_hi(trip, ch, j):
                u = 3 * ch + j
                act.wait_ge(landed[(DENSE + u) % LAND], trip * (16 * UPE // LAND) + 16 * ((DENSE + u) // LAND + 1))
                if j < 2:
                    n = DENSE + 2 * ch + j
                    act.wait_ge(used, trip * (2 * NCH) + n - RING + 1)
                    act.copy(w_hi[n % RING][:], land[(DENSE + u) % LAND][:]).then_inc(hi_done, 1)
                else:
                    act.wait_ge(d_used, trip * NCH + ch + 1)
                    act.copy(d_hi[ch % 2][:], land[(DENSE + u) % LAND][:]).then_inc(d_hi_done, 1)

            def h_tok(h):
                if h == 0:
                    act.wait_ge(kv_stored, 80)
                act.wait_ge(htok_done, h + 1)
                for i, (t0, nt) in enumerate(TT):
                    act.copy(H_tok[0:nt, i, 512 * h:512 * h + 512], bank[4 + i][0:nt, :]).then_inc(htok_ready, 1)

            for k in range(KT_D):
                act.wait_ge(x_attn, k + 1)
                square(4, X, k)
                if k % 2 and k < KT_D - 1:
                    expert_hi(0, *FIRST_UNITS[k // 2])
                if k == 5:
                    h_tok(0)
            act.wait_ge(lg_done, 1)
            act.activation(rt[:], STAT[:, 0:3], ACT.Sqrt, bias=c("eps")).then_inc(sd_ready, 1)
            act.wait_ge(lg_ready, 1)
            act.activation(lg[:, 2], lg[:, 3], ACT.Exp).then_inc(ex_ready, 1)
            h_tok(1)
            expert_hi(0, *FIRST_UNITS[3])
            expert_hi(0, 0, 2)
            expert_hi(0, 1, 2)
            act.wait_ge(route_ready, 1)
            n_trips = act.value_load(trips[0:1, 1:2], min_val=NE, max_val=PASSES * NE)

            def xe_split(first, h):
                act.wait_ge(gathered, first + h + 1)
                act.copy(xe_hi[:, 512 * h:512 * h + 512], bank[4 + h][:, :]).then_inc(xe_hi_ready, 1)

            xe_split(0, 0)
            xe_split(0, 1)
            with act.Fori(0, n_trips) as trip:
                for ch in range(NCH):
                    act.wait_ge(used, trip * (2 * NCH) + DENSE + 2 * ch + 2)
                    act.activation(silu_g[:], bank[ch % 2][:, 0:CH], ACT.Silu).then_inc(esilu_ready, 1)
                    if ch == GATES_AT + 1:
                        act.wait_ge(PT_done, trip + 1)
                        act.copy(PT[:, :], bank[7][:, 0:T]).then_inc(PT_ready, 1)
                    if 2 <= ch + 1 < NCH:
                        expert_hi(trip, ch + 1, 2)
                    elif ch + 1 == NCH:
                        with act.If(trip < n_trips - 1):
                            xe_split((trip + 1) * 2, 0)
                    act.wait_ge(heT_done, trip * NCH + ch + 1)
                    act.wait_ge(d_used, trip * NCH + ch + 2)
                    act.copy(heT_hi[:], bank[6][:, 0:CH]).then_inc(heT_hi_ready, 1)
                    if ch + 2 < NCH:
                        expert_hi(trip, ch + 2, 0)
                        expert_hi(trip, ch + 2, 1)
                    elif ch + 2 == NCH:
                        with act.If(trip < n_trips - 1):
                            expert_hi(trip, ch + 2, 0)
                            expert_hi(trip, ch + 2, 1)
                    else:
                        with act.If(trip < n_trips - 1):
                            xe_split((trip + 1) * 2, 1)
                            expert_hi(trip, ch + 2, 0)
                            expert_hi(trip, NCH, 2)
                            expert_hi(trip, ch + 2, 1)
                act.wait_ge(d_used, trip * NCH + NCH + 2)
                act.copy(oe[:, 0:512], bank[2][:, :]).then_inc(oe_ready, 1)
                with act.If(trip < n_trips - 1):
                    expert_hi(trip, NCH + 1, 2)

        @block.vector
        def _(dve):
            count = [0]

            def seq(ins):
                count[0] += 1
                ins.then_inc(dve_seq, 1)
                dve.wait_ge(dve_seq, count[0])

            n_lo = 0

            def lo_to(m):
                nonlocal n_lo
                while n_lo < min(m, DENSE):
                    n = n_lo
                    cols = DOWN_LAST * P if n in (U_DOWN[0] + DOWN_UNITS - 1, U_DOWN[1] + DOWN_UNITS - 1) else UNIT
                    dve.wait_ge(hi_done, n + 1)
                    dve.tensor_tensor(w_lo[n % RING][:, 0:cols], land[n % LAND][:, 0:cols],
                                      w_hi[n % RING][:, 0:cols].bitcast(F32), ALU.subtract).then_inc(split, 1)
                    n_lo += 1

            def inverse_root(q):
                dve.wait_ge(sd_ready, q + 1)
                dve.reciprocal(rr[:], sd[:]).then_inc(rr_ready, 1)
                dve.wait_ge(rr_ready, q + 1)

            def h_lo_odd(a, k, hi, lo):
                m = h_number(a, k)
                dve.wait_ge(h_hi_ready, m + 1)
                dve.tensor_tensor(lo[:, k, :], raw[:, m % RAW, :], hi[:, k, :].bitcast(F32),
                                  ALU.subtract).then_inc(h_ready[1], 1)

            def gained(a, gain, k):
                m = h_number(a, k)
                dve.wait_ge(h_ready[m % 2], m // 2 - 1)
                dve.tensor_scalar(raw[:, m % RAW, :], X[:, k, :], v(gain, k), None, ALU.mult).then_inc(raw_ready, 1)

            seq(dve.memset(Up[:, :, 0:CW - 1], 0.0))
            dve.wait_ge(in_vec, 16)
            seq(dve.tensor_scalar(g_q8[:], v("g_q"), HD ** -0.5, None, ALU.mult))
            lo_to(1)
            inverse_root(0)
            for k in range(KT_D):
                m = h_number(0, k)
                if m >= RAW:
                    dve.wait_ge(h_ready[m % 2], m // 2 - 1)
                dve.scalar_tensor_tensor(out=raw[:, m % RAW, :], in0=X[:, k, :], scalar=v("g_conv", k), in1=rr[:],
                                         op0=ALU.mult, op1=ALU.mult).then_inc(raw_ready, 1)
                if k % 2 and k >= 3:
                    h_lo_odd(0, k - 2, H_hi, H_lo)
            h_lo_odd(0, KT_D - 1, H_hi, H_lo)
            lo_to(RING)

            tap_done = {}

            def tap(j, w):
                acc = odd[:] if w % 2 else C[:, j, 0:SEQ]
                x = Up[:, j, w:w + SEQ]
                if w == 0:
                    dve.wait_ge(u_ready, j + 1)
                    ins = dve.tensor_scalar(acc, x, w_dw[:, j, w:w + 1], v("b_dw", j), ALU.mult, ALU.add)
                elif w == 1:
                    if j > POOL_CONV:
                        dve.wait_ge(c_ready, j - POOL_CONV)
                    ins = dve.tensor_scalar(acc, x, w_dw[:, j, w:w + 1], None, ALU.mult)
                else:
                    dve.wait_ge(dve_seq, tap_done[w % 2])
                    ins = dve.scalar_tensor_tensor(out=acc, in0=x, scalar=w_dw[:, j, w:w + 1], in1=acc,
                                                   op0=ALU.mult, op1=ALU.add)
                ins.then_inc(dve_seq, 1)
                count[0] += 1
                tap_done[w % 2] = count[0]
                if w == CW - 1:
                    dve.wait_ge(dve_seq, count[0])
                    dve.tensor_tensor(C[:, j, 0:SEQ], C[:, j, 0:SEQ], odd[:], ALU.add).then_inc(c_ready, 1)

            def sample_conv(j):
                out = C[:, j, SEQ:T]
                dve.wait_ge(win_ready, j + 1)
                seq(dve.tensor_reduce(out.rearrange("p (b t) -> p b t", b=NB), win[:], AX.X, ALU.add))
                dve.tensor_scalar(out, out, v("b_dw", j), None, ALU.add).then_inc(cs_ready, 1)

            taps = [(j, w) for j in range(POOL_CONV, DVE_CONV) for w in range(CW)]
            dve.wait_ge(in_state, 16)
            dve.wait_ge(in_dw, 16)
            for j in range(KT_D):
                lo_to(j + RING)
                dve.wait_ge(sig_ready, j + 1)
                dve.scalar_tensor_tensor(out=Us[:, j, :, CW - 1:CW - 1 + DS],
                                         in0=bank[2 * (j % 2)][:, SEQ:T].rearrange("p (b t) -> p b t", b=NB),
                                         scalar=v("b_a", j),
                                         in1=gate_s[:, j % 2, SEQ:T].rearrange("p (b t) -> p b t", b=NB),
                                         op0=ALU.add, op1=ALU.mult)
                dve.scalar_tensor_tensor(out=Up[:, j, CW - 1:CW - 1 + SEQ], in0=bank[2 * (j % 2)][:, 0:SEQ],
                                         scalar=v("b_a", j), in1=gate_s[:, j % 2, 0:SEQ],
                                         op0=ALU.add, op1=ALU.mult).then_inc(u_ready, 1)
                if j == 1:
                    dve.wait_ge(rel_sum, 1)
                    dve.tensor_copy(rb[:], bank[5][0:NH, 0:RLEN]).then_inc(rb_ready, 1)
                if j >= 1:
                    sample_conv(j - 1)
                if j >= POOL_CONV:
                    for t in taps[TAPS_BETWEEN * (j - 1):TAPS_BETWEEN * j]:
                        tap(*t)
            sample_conv(KT_D - 1)
            for t in taps[TAPS_BETWEEN * (KT_D - 1):]:
                tap(*t)
            dve.wait_ge(mean_ready, 1)
            dve.wait_ge(c_ready, DVE_CONV - POOL_CONV)
            dve.wait_ge(cg_ready, POOL_CONV)
            dve.wait_ge(cs_ready, KT_D)
            dve.wait_ge(cp_ready, PE_CONV)
            for k in range(KT_D):
                dve.tensor_tensor(C[:, k, :], C[:, k, :], MEAN[:, 0:T], ALU.subtract).then_inc(xc_ready, 1)
            lo_to(U_PW2 + RING)
            inverse_root(1)
            dve.wait_ge(xc_ready, KT_D)
            for k in range(KT_D):
                dve.scalar_tensor_tensor(out=C[:, k, :], in0=C[:, k, :], scalar=v("g_ln", k), in1=rr[:],
                                         op0=ALU.mult, op1=ALU.mult).then_inc(ln_ready, 1)
            for k in range(1, KT_D, 2):
                h_lo_odd(1, k, H_hi, H_lo)
            for d in range(KT_D):
                dve.wait_ge(pw2_done, d + 1)
                dve.scalar_tensor_tensor(out=X[:, d, :], in0=bank[d % 4][:, 0:T], scalar=v("b_pw2", d),
                                         in1=X[:, d, :], op0=ALU.add, op1=ALU.add).then_inc(x_conv, 1)
                dve.wait_ge(x_conv, d + 1)
                gained(2, "g_ffn", d)
                if d % 2 and d >= 3:
                    h_lo_odd(2, d - 2, G_hi, G_lo)
                if d % 2 and d < KT_D - 1:
                    lo_to(U_PW2 + RING + d // 2 + 1)
            h_lo_odd(2, KT_D - 1, G_hi, G_lo)
            inverse_root(2)
            lo_to(U_GU[0] + RING)
            for half in range(2):
                for i in range(FH):
                    f = FH * half + i
                    dve.wait_ge(used, U_GU[half] + i + 1)
                    if f >= 2:
                        dve.wait_ge(a_raw, f - 1)
                    dve.tensor_tensor(gate_f[:, f % 2, :], bank[2 * (f % 2)][:, 0:T], rr[:],
                                      ALU.mult).then_inc(g_scaled, 1)
                    if i < FH - 1:
                        lo_to(U_GU[half] + i + RING)
                    dve.wait_ge(silu_ready, f + 1)
                    if f >= RAW:
                        dve.wait_ge(a_ready, f - RAW + 1)
                    else:
                        m = h_number(2, KT_D - RAW + f)
                        dve.wait_ge(h_ready[m % 2], m // 2 + 1)
                    dve.tensor_tensor(raw[:, f % RAW, :], gate_f[:, f % 2, :], bank[2 * (f % 2) + 1][:, 0:T],
                                      ALU.mult).then_inc(a_raw, 1)
                for d in range(KT_D):
                    lo_to(U_DOWN[half] + min(DOWN_UNITS, FH * d // BPU) + RING)
                    dve.wait_ge(down_done, KT_D * half + d + 1)
                    if KT_D * half + d >= 1:
                        dve.wait_ge(x_ffn, KT_D * half + d)
                    seq(dve.tensor_tensor(sd[:], bank[4 + d % 2][:, 0:T], rr[:], ALU.mult))
                    dve.tensor_tensor(X[:, d, :], sd[:], X[:, d, :], ALU.add).then_inc(x_ffn, 1)
                    if half == 1:
                        dve.wait_ge(x_ffn, KT_D + d + 1)
                        if d == 0:
                            dve.wait_ge(a_ready, FT)
                        gained(3, "g_kv", d)
                        gained(4, "g_attn", d)
                        if d >= 1:
                            h_lo_odd(4, d - 1, G_hi, G_lo)
                if half == 0:
                    lo_to(U_GU[1] + 3)
            h_lo_odd(4, KT_D - 1, G_hi, G_lo)
            inverse_root(3)
            lo_to(U_K + RING)

            def head_norm(i, out, gain):
                dve.wait_ge(kq_sd, i + 1)
                seq(dve.reciprocal(raw[:, i % 2, :], raw[:, 2 + i % 2, :]))
                dve.scalar_tensor_tensor(out=out, in0=out, scalar=gain, in1=raw[:, i % 2, :],
                                         op0=ALU.mult, op1=ALU.mult).then_inc(kq_ready, 1)

            dve.wait_ge(h_ready[0], 5 * KT_D // 2)
            dve.wait_ge(h_ready[1], 5 * KT_D // 2)
            head_norm(0, K[:, 0, :], v("g_k"))
            head_norm(1, K[:, 1, :], v("g_k"))
            lo_to(U_V + RING)
            dve.wait_ge(in_kc, 16)
            dve.wait_ge(kq_ready, 2)
            dve.tensor_copy(KC[:, :, :, WIN:WIN + DS],
                            K[:, :, SEQ:T].rearrange("p n (b t) -> p n b t", b=NB)).then_inc(kc_ready, 1)
            for t in range(KT_D - 1):
                head_norm(2 + t, Q[:, t, :], g_q8[:])
                if t < KT_D - 2:
                    lo_to(U_Q + t // 2 + RING)

            def soft_args(s):
                sm = small[:, s % 2, :]
                dve.wait_ge(sc_done, s + 1)
                if STEPS[s] is None:
                    dve.wait_ge(in_bias_s, 64)
                    own = c("own_new").rearrange("p (a b t) -> p a b t", a=4, b=NB)
                    seq(dve.tensor_tensor(bias_o[:], own, bias_n.unsqueeze(1).unsqueeze(1).to_broadcast([P, 4, NB, DS]), ALU.add))
                    for h in range(2):
                        src = bank[2 * (s % 2) + h][:, 0:2 * (WIN + NS)].rearrange("p (a s) -> p a s", a=2)
                        dve.tensor_tensor(SS[:, 2 * h:2 * h + 2, 0:WIN], src[:, :, 0:WIN],
                                          bias_c.unsqueeze(1).to_broadcast([P, 2, WIN]), ALU.add)
                        last = dve.tensor_tensor(SS[:, 2 * h:2 * h + 2, WIN:WIN + NS], src[:, :, WIN:WIN + NS],
                                                 bias_o[:, 2 * h:2 * h + 2].rearrange("p a b t -> p a (b t)"), ALU.add)
                    last.then_inc(s_ready, 1)
                    dve.wait_ge(s_ready, s + 1)
                    seq(dve.tensor_reduce(sm[:, 0:4], SS[:], AX.X, ALU.max))
                    seq(dve.tensor_scalar(sm[:, 0:4], sm[:, 0:4], v("sink_row"), None, ALU.max))
                    dve.tensor_scalar(sm[:, 4:8], sm[:, 0:4], -1.0, None, ALU.mult).then_inc(nm_ready, 1)
                    dve.wait_ge(nm_ready, s + 1)
                    dve.tensor_scalar(sm[:, 12:16], sm[:, 4:8], v("sink_row"), None, ALU.add).then_inc(es_arg, 1)
                    return
                n, b = STEPS[s]
                w = (b + 1) * P
                dve.wait_ge(in_bias[n % 2], 16 * (n // 2 + 1))
                if s >= 2:
                    dve.wait_ge(pT_done, TURNS[s - 1])
                for h in range(b + 1):
                    gs = GR // (b + 1)
                    a = 512 * h
                    last = dve.tensor_tensor(S[:, s % 2, a:a + 512].rearrange("p (g s) -> p g s", g=gs),
                                             bank[2 * (s % 2) + h][:, :].rearrange("p (g s) -> p g s", g=gs),
                                             bias[:, n % 2, gs * h:gs * h + gs, 2 * P - w:2 * P], ALU.add)
                last.then_inc(s_ready, 1)
                dve.wait_ge(s_ready, s + 1)
                seq(dve.tensor_reduce(sm[:, 0:4], S[:, s % 2, 0:GR * w].rearrange("p (g s) -> p g s", g=GR),
                                      AX.X, ALU.max))
                seq(dve.tensor_tensor(sm[:, 0:4], sm[:, 0:4], v("sinks", GR * n, GR), ALU.max))
                dve.tensor_scalar(sm[:, 4:8], sm[:, 0:4], -1.0, None, ALU.mult).then_inc(nm_ready, 1)
                dve.tensor_tensor(sm[:, 12:16], v("sinks", GR * n, GR), sm[:, 0:4],
                                  ALU.subtract).then_inc(es_arg, 1)

            def normalise(s):
                sm = small[:, s % 2, :]
                dve.wait_ge(p_ready, s + 1)
                seq(dve.tensor_tensor(sm[:, 20:24], sm[:, 8:12], sm[:, 16:20], ALU.add))
                seq(dve.reciprocal(sm[:, 20:24], sm[:, 20:24]))
                for g in range(GR):
                    if STEPS[s] is None:
                        part = SS[:, g, :]
                    else:
                        w = (STEPS[s][1] + 1) * P
                        part = S[:, s % 2, w * g:w * g + w]
                    last = dve.tensor_scalar(part, part, sm[:, 20 + g:21 + g], None, ALU.mult)
                last.then_inc(pn_ready, 1)

            def o_lo(s):
                dve.wait_ge(o_hi_ready, OUT_STEPS.index(s) + 1)
                if STEPS[s] is None:
                    for ng in range(2):
                        for i in range(2):
                            rows = slice(HD * i, HD * i + HD)
                            last = dve.tensor_tensor(sample_rows(H_lo, rows, ng), sample_out(rows, ng, i),
                                                     sample_rows(H_hi, rows, ng).bitcast(F32), ALU.subtract)
                else:
                    n, b = STEPS[s]
                    ng = n // 2
                    last = dve.tensor_tensor(H_lo[:, GR * ng:GR * ng + GR, P * b:P * b + P],
                                             bank[6 + b][:, :].rearrange("p (g q) -> p g q", g=GR),
                                             H_hi[:, GR * ng:GR * ng + GR, P * b:P * b + P].bitcast(F32),
                                             ALU.subtract)
                last.then_inc(o_ready, 1)

            soft_args(0)
            for s in range(len(STEPS)):
                if s + 1 < len(STEPS):
                    soft_args(s + 1)
                normalise(s)
                if s == 0:
                    head_norm(2 + KT_D - 1, Q[:, KT_D - 1, :], g_q8[:])
                if s == 1:
                    lo_to(DENSE)
                if s - 1 in OUT_STEPS:
                    o_lo(s - 1)
            o_lo(len(STEPS) - 1)
            def expert_lo(trip, ch, j):
                n, slot = DENSE + 2 * ch + j, (DENSE + 3 * ch + j) % LAND
                dve.wait_ge(hi_done, trip * (2 * NCH) + n + 1)
                dve.tensor_tensor(w_lo[n % RING][:], land[slot][:], w_hi[n % RING][:].bitcast(F32),
                                  ALU.subtract).then_inc(split, 1)

            dve.wait_ge(kv_stored, 80)
            dve.memset(oe[:], 0.0).then_inc(oe_ready, 2)
            dve.memset(PT[:], 0.0).then_inc(PT_ready, 1)
            for d in range(KT_D):
                dve.wait_ge(wo_done, d + 1)
                dve.tensor_tensor(X[:, d, :], bank[d % 4][:, 0:T], X[:, d, :], ALU.add).then_inc(x_attn, 1)
                dve.wait_ge(x_attn, d + 1)
                dve.tensor_scalar(Hm[:, d, :], X[:, d, :], v("g_moe", d), None, ALU.mult).then_inc(hm_ready, 1)
                if d % 2 and d < KT_D - 1:
                    expert_lo(0, *FIRST_UNITS[d // 2])
            LG, SEL, EX, DIFF, TMP, COMB = (lg[:, i] for i in range(6))
            dve.wait_ge(sd_ready, 5)
            seq(dve.reciprocal(rt[:], rt[:]))
            dve.wait_ge(lg_done, 1)
            seq(dve.tensor_tensor(LG, STAT[:, 8:8 + 3 * NE].rearrange("p (i e) -> p i e", i=3),
                                  rt[:].unsqueeze(2).to_broadcast([P, 3, NE]), ALU.mult))
            seq(dve.tensor_reduce(top[:, 0:3], LG, AX.X, ALU.max))
            dve.tensor_tensor(DIFF, LG, top[:, 0:3].unsqueeze(2).to_broadcast([P, 3, NE]),
                              ALU.subtract).then_inc(lg_ready, 1)
            other = LG.unsqueeze(2).to_broadcast([P, 3, NE, NE])
            mine = LG.unsqueeze(3).to_broadcast([P, 3, NE, NE])
            tie = c("tie").rearrange("p (e f) -> p e f", e=NE).unsqueeze(1).to_broadcast([P, 3, NE, NE])
            dve.tensor_tensor(cmp_[:, 0], other, mine, ALU.is_gt)
            seq(dve.tensor_tensor(cmp_[:, 1], other, mine, ALU.is_equal))
            seq(dve.tensor_tensor(cmp_[:, 1], cmp_[:, 1], tie, ALU.mult))
            seq(dve.tensor_tensor(cmp_[:, 0], cmp_[:, 0], cmp_[:, 1], ALU.add))
            seq(dve.tensor_reduce(TMP, cmp_[:, 0], AX.X, ALU.add))
            dve.tensor_scalar(SEL, TMP, TOP_K - 0.5, None, ALU.is_lt).then_inc(sel_ready, 1)
            dve.wait_ge(sel_ready, 1)
            dve.wait_ge(ex_ready, 1)
            seq(dve.tensor_tensor(EX, EX, SEL, ALU.mult))
            seq(dve.tensor_reduce(top[:, 4:7], EX, AX.X, ALU.add))
            seq(dve.reciprocal(top[:, 4:7], top[:, 4:7]))
            seq(dve.tensor_tensor(COMB, EX, top[:, 4:7].unsqueeze(2).to_broadcast([P, 3, NE]), ALU.mult))
            seq(dve.tensor_scalar(TMP, SEL, -NOT_HERE, NOT_HERE, ALU.mult, ALU.add))
            dve.wait_ge(pos_done, 1)
            dve.tensor_tensor(TMP[:, 0:2, :], TMP[:, 0:2, :], STAT[:, 32:32 + 2 * NE].rearrange("p (i e) -> p i e", i=2), ALU.add)
            seq(dve.tensor_tensor(TMP[0:NS, 2, :], TMP[0:NS, 2, :], STAT[0:NS, 32 + 2 * NE:32 + 3 * NE], ALU.add))
            for p in range(PASSES):
                dve.tensor_copy(gate_of[:, :, NE * p:NE * p + NE], COMB)
                last = dve.tensor_scalar(slot_of[:, :, NE * p:NE * p + NE], TMP, -float(SLOTS * p), None, ALU.add)
            seq(last)
            def place(t):
                for i, (t0, nt) in enumerate(TT):
                    last = dve.tensor_scalar(pick[0:nt, i, :], c("iota")[0:nt, :], slot_of[0:nt, i, bass.ds(t, 1)],
                                             rt[0:nt, i:i + 1], ALU.is_equal, ALU.mult)
                last.then_inc(P_ready, 1)
                for i, (t0, nt) in enumerate(TT):
                    last = dve.tensor_scalar(PG[0:nt, i, :], c("iota")[0:nt, :], slot_of[0:nt, i, bass.ds(t, 1)],
                                             gate_of[0:nt, i, bass.ds(t, 1)], ALU.is_equal, ALU.mult)
                last.then_inc(PG_ready, 1)

            place(0)
            seq(dve.tensor_reduce(top[:, 8:9], STAT[:, 64:64 + NE], AX.X, ALU.max))
            seq(dve.tensor_scalar(top[:, 9:10], top[:, 8:9], SLOTS + 0.5, 1.0, ALU.is_gt, ALU.add))
            seq(dve.tensor_scalar(top[:, 10:11], top[:, 8:9], 2 * SLOTS + 0.5, None, ALU.is_gt))
            seq(dve.tensor_tensor(top[:, 11:12], top[:, 9:10], top[:, 10:11], ALU.add))
            seq(dve.tensor_scalar(top[:, 12:13], top[:, 11:12], float(NE), None, ALU.mult))
            dve.tensor_copy(trips[0:1, 0:2], top[0:1, 11:13]).then_inc(route_ready, 1)
            dve.wait_ge(route_ready, 1)
            n_trips = dve.value_load(trips[0:1, 1:2], min_val=NE, max_val=PASSES * NE)

            def xe_rest(first, h):
                dve.wait_ge(xe_hi_ready, first + h + 1)
                dve.tensor_tensor(xe_lo[:, 512 * h:512 * h + 512], bank[4 + h][:, :],
                                  xe_hi[:, 512 * h:512 * h + 512].bitcast(F32), ALU.subtract).then_inc(xe_ready, 1)

            def add_back(trip, k, src=bank[7]):
                dve.wait_ge(y_done, trip * KT_D + k + 1)
                dve.tensor_tensor(X[:, k, :], src[:, 0:T], X[:, k, :], ALU.add).then_inc(y_added, 1)

            expert_lo(0, *FIRST_UNITS[3])
            xe_rest(0, 0)
            xe_rest(0, 1)
            with dve.Fori(0, n_trips) as trip:
                for ch in range(NCH):
                    dve.wait_ge(esilu_ready, trip * NCH + ch + 1)
                    dve.tensor_tensor(he[:], silu_g[:], bank[ch % 2][:, CH:2 * CH], ALU.mult).then_inc(he_ready, 1)
                    if ch == GATES_AT + 1:
                        with dve.If(trip < n_trips - 1):
                            dve.wait_ge(PT_done, trip + 1)
                            place(trip + 1)
                    if ch == NCH - 1:
                        with dve.If(trip < n_trips - 1):
                            xe_rest((trip + 1) * 2, 0)
                    dve.wait_ge(heT_hi_ready, trip * NCH + ch + 1)
                    dve.tensor_tensor(heT_lo[:], bank[6][:, 0:CH], heT_hi[:].bitcast(F32),
                                      ALU.subtract).then_inc(heT_ready, 1)
                    if ch + 2 < NCH:
                        expert_lo(trip, ch + 2, 0)
                        expert_lo(trip, ch + 2, 1)
                    elif ch + 2 == NCH:
                        with dve.If(trip < n_trips - 1):
                            expert_lo(trip, ch + 2, 0)
                            expert_lo(trip, ch + 2, 1)
                    else:
                        with dve.If(trip < n_trips - 1):
                            xe_rest((trip + 1) * 2, 1)
                            expert_lo(trip, ch + 2, 0)
                            expert_lo(trip, ch + 2, 1)
                    if 1 <= ch <= KT_D:
                        add_back(trip, ch - 1)
                dve.wait_ge(d_used, trip * NCH + NCH + 2)
                dve.tensor_copy(oe[:, 512:1024], bank[3][:, :]).then_inc(oe_ready, 1)
            for k in range(KT_D):
                add_back(n_trips, k, bank[4 + k % 4])

        @block.gpsimd
        def _(pool):
            def h_lo_even(a, tiles, hi, lo):
                for k in tiles:
                    pool.wait_ge(h_hi_ready, h_number(a, k) + 1)
                    pool.tensor_tensor(lo[:, k, :], raw[:, h_number(a, k) % RAW, :], hi[:, k, :].bitcast(F32),
                                       ALU.subtract).then_inc(h_ready[0], 1)

            def diagonals(m):
                for g, taps in enumerate(GROUPS):
                    if m >= 1:
                        pool.wait_ge(diag_used, len(GROUPS) * (m - 1) + g + 1)
                    pool.tensor_tensor(diag[:, g, 0:len(taps), :],
                                       ident.unsqueeze(1).to_broadcast([P, len(taps), P]),
                                       w_dw[:, DVE_CONV + m, taps[0]:taps[-1] + 1].unsqueeze(2).to_broadcast(
                                           [P, len(taps), P]), ALU.mult).then_inc(diag_ready, 1)

            pool.dma_start(w_dw[:], io["w_dw"]).then_inc(in_dw, 16)
            pool.dma_start(relb[:], io["relb"]).then_inc(in_rel, 16)
            pool.dma_start(buckets[:], io["buckets"]).then_inc(in_rel, 16)
            pool.wait_ge(landed[0], 16)
            pool.dma_start(Us[:], io["state"]).then_inc(in_state, 16)
            h_lo_even(0, range(0, KT_D, 2), H_hi, H_lo)
            pool.wait_ge(in_con, 16)
            pool.wait_ge(in_dw, 16)
            diagonals(0)

            def add_tap(w):
                pool.wait_ge(tap_ready, w + 1)
                if w >= 2:
                    pool.wait_ge(tap_added, w - 1)
                out = C[:, 0, 0:SEQ]
                pool.tensor_tensor(out, out, prod[:, w % 4, :], ALU.add).then_inc(cg_ready if w == CW - 1 else tap_added, 1)

            for j in range(KT_D):
                pool.wait_ge(u_ready, j + 1)
                if j >= 1:
                    pool.wait_ge(cs_ready, j)
                first = Us[:, j, :, 0:1]
                windows = bass.AP(tensor=first.tensor, offset=first.offset,
                                  ap=[list(first.ap[0]), [DS + CW - 1, NB], [1, DS], [1, CW]])
                pool.tensor_tensor(win[:], windows, w_dw[:, j, :].unsqueeze(1).unsqueeze(1).to_broadcast(
                    [P, NB, DS, CW]), ALU.mult).then_inc(win_ready, 1)
                for w in range(max(4 * j, 1), min(4 * j + 4, CW)):
                    add_tap(w)
                if j == 1:
                    pool.wait_ge(rb_ready, 1)
                    per_head = P * RLEN
                    pool.dma_start(bass.AP(tensor=io["rel_rows"].tensor, offset=0,
                                           ap=[[per_head, NH], [RLEN, P], [1, RLEN]]),
                                   rb[:].unsqueeze(1).to_broadcast([NH, P, RLEN])).then_inc(rb_stored, 16)
            for m in range(1, PE_CONV):
                diagonals(m)
            pool.dma_start(io["conv_p"], Up[:, :, SEQ:SEQ + CW - 1]).then_inc(conv_stored, 16)
            pool.dma_start(io["conv_s"], Us[:]).then_inc(conv_stored, 16)
            h_lo_even(1, range(0, KT_D, 2), H_hi, H_lo)
            h_lo_even(2, range(0, KT_D, 2), G_hi, G_lo)
            for f in range(FT):
                pool.wait_ge(a_hi_ready, f + 1)
                pool.tensor_tensor(A_lo[:, f % (FH + 1), :], raw[:, f % RAW, :],
                                   A_hi[:, f % (FH + 1), :].bitcast(F32), ALU.subtract).then_inc(a_ready, 1)
            h_lo_even(3, range(KT_D), H_hi, H_lo)
            pool.dma_start(io["v_s"][:, 0:WIN - DS, :].rearrange("b s n -> s b n"), io["vc"][DS:WIN, :, :]).then_inc(kv_stored, 16)
            pool.wait_ge(rr_ready, 4)
            for i in range(2 + KT_D):
                dst = K[:, i, :] if i < 2 else Q[:, i - 2, :]
                pool.wait_ge(kq_copied, i + 1)
                pool.tensor_tensor(dst, dst, rr[:], ALU.mult).then_inc(kq_scaled, 1)
            pool.wait_ge(kq_ready, 2 + KT_D)
            pool.memset(QZ, 0.0).then_inc(qz_zero, 1)
            pool.wait_ge(qz_zero, 1)
            for ng in range(2):
                for i in range(2):
                    rows = slice(HD * i, HD * i + HD)
                    a = (2 * ng + i) * GR * DS
                    last = pool.tensor_copy(QZ[rows, ng, :, a:a + GR * DS].rearrange("p b (g t) -> p b g t", g=GR),
                                            sample_rows(Q, rows, ng).rearrange("p g b t -> p b g t"))
            last.then_inc(qz_ready, 1)
            pool.wait_ge(kc_ready, 1)
            pool.wait_ge(v_ready, 1)
            pool.dma_start(io["k_p"], K[:, :, P:2 * P]).then_inc(kv_stored, 16)
            pool.dma_start(io["k_s"], KC[:]).then_inc(kv_stored, 16)
            pool.dma_start(io["v_p"], V[:, 1, :]).then_inc(kv_stored, 16)
            pool.dma_start(bass.AP(tensor=io["v_s"].tensor, offset=(WIN - DS) * 256,
                                   ap=[[WIN * 256, NB], [256, DS], [1, 256]]), V[0:NS, 2, :]).then_inc(kv_stored, 16)


            def expert_lo(trip, ch):
                slot = (DENSE + 3 * ch + 2) % LAND
                pool.wait_ge(d_hi_done, trip * NCH + ch + 1)
                pool.tensor_tensor(d_lo[ch % 2][:], land[slot][:], d_hi[ch % 2][:].bitcast(F32),
                                   ALU.subtract).then_inc(d_split, 1)

            pool.sem_inc(d_split, 2)
            expert_lo(0, 0)
            expert_lo(0, 1)
            pool.wait_ge(route_ready, 1)
            n_trips = pool.value_load(trips[0:1, 1:2], min_val=NE, max_val=PASSES * NE)
            with pool.Fori(0, n_trips) as trip:
                for ch in range(NCH):
                    if 2 <= ch + 1 < NCH:
                        expert_lo(trip, ch + 1)
                with pool.If(trip < n_trips - 1):
                    expert_lo(trip, NCH)
                    expert_lo(trip, NCH + 1)



def _t5_bucket(dist):
    n = np.maximum(dist, 0)
    exact = 16
    large = exact + (np.log(np.maximum(n, 1) / exact) / np.log(128 / exact) * (32 - exact)).astype(np.int32)
    return np.where(n < exact, n, np.minimum(large, 31)).astype(np.int32)


def _constants():
    con = np.zeros((P, NCON), np.float32)

    def put(name, a):
        lo, hi = CON[name]
        con[:, lo:hi] = a

    part = np.arange(P)
    put("ident", np.eye(P))
    put("mean_d", 1.0 / D)
    put("mean_head", (part[:, None] // HD == part[None, :] // HD) / HD)
    put("ones", 1.0)
    put("before", part[:, None] < part[None, :])
    put("iota", np.arange(SLOTS)[None, :])
    pair, seq_of_col = np.arange(4)[None, :, None], (np.arange(NS) // DS)[None, None, :]
    own = (2 * pair + (part // 64)[:, None, None]) == seq_of_col
    put("own_new", np.where(own, 0.0, MASKED).reshape(P, 4 * NS))
    put("tie", (np.arange(NE)[None, :] < np.arange(NE)[:, None]).reshape(1, -1))
    put("eps", EPS)
    dist = 255 - np.arange(RLEN)
    valid = (dist >= 0) & (dist < WIN)
    buckets = np.zeros((NREL, RLEN), np.float32)
    buckets[_t5_bucket(dist)[valid], np.arange(RLEN)[valid]] = 1.0
    buckets[NREL - 1] = np.where(valid, 0.0, MASKED)
    return con, buckets


def _blocks(w):
    r, n = w.shape
    return w.reshape(r // P, P, n // P, P).transpose(0, 2, 1, 3)


def _layout(i):
    f = {k: np.asarray(a) for k, a in i.items()}
    ch = lambda a: a.reshape(KT_D, P).T
    x = np.concatenate([f["x_prompt"].reshape(SEQ, D), f["x_sample"].reshape(NS, D)])
    x = x.reshape(T, KT_D, P).transpose(2, 1, 0)
    parts = {
        "g_conv": ch(f["g_conv_norm"]), "b_a": ch(f["b_pw1"][0, :D]), "b_g": ch(f["b_pw1"][0, D:]),
        "b_dw": ch(f["b_dw"]), "g_ln": ch(f["g_ln"]), "b_ln": ch(f["b_ln"]), "b_pw2": ch(f["b_pw2"]),
        "g_ffn": ch(f["g_ffn_norm"]), "g_kv": ch(f["g_kv_norm"]), "g_attn": ch(f["g_attn_norm"]),
        "g_moe": ch(f["g_moe_norm"]), "g_k": np.tile(f["g_k_norm"], 2)[:, None],
        "g_q": np.tile(f["g_q_norm"][0], 2)[:, None],
        "sink_row": np.tile(np.repeat(f["sinks"][0], DS), 2)[:, None],
        "sinks": np.tile(f["sinks"][0][None, :], (P, 1)),
        "router": f["w_router"][0].reshape(KT_D, P, NE).transpose(1, 0, 2).reshape(P, -1),
    }
    vec = np.concatenate([parts[n] for n in VEC], axis=1)
    heads = [GR * (2 * ng + i) + g for ng in range(2) for g in range(GR) for i in range(2)]
    perm = np.concatenate([np.arange(HD) + HD * h for h in heads])
    pw1, pw2 = _blocks(f["w_pw1"][0]), _blocks(f["w_pw2"][0])
    wg, wu, wdn = _blocks(f["w_gate"][0]), _blocks(f["w_up"][0]), _blocks(f["w_down"][0])
    wk = _blocks(f["w_kv"][:, :NKV * HD])
    wv = f["w_kv"][:, NKV * HD:]
    wq = _blocks(f["w_q"][0][:, perm])
    wo = _blocks(f["w_o"][0][perm, :])
    unit = lambda b: b.reshape(BPU, P, P).transpose(1, 0, 2).reshape(P, UNIT)
    units = [unit(np.concatenate([pw1[:, j], pw1[:, KT_D + j]])) for j in range(KT_D)]
    two = lambda w: [unit(np.concatenate([w[:, 2 * d], w[:, 2 * d + 1]])) for d in range(w.shape[1] // 2)]
    units += two(pw2)
    for half in range(2):
        fs = range(FH * half, FH * half + FH)
        units += [unit(np.concatenate([wg[:, t], wu[:, t]])) for t in fs]
        b = np.concatenate([wdn[FH * half:FH * half + FH, d] for d in range(KT_D)])
        b = np.concatenate([b, np.zeros((DOWN_UNITS * BPU - len(b), P, P), np.float32)])
        units += [unit(b[BPU * u:BPU * u + BPU]) for u in range(DOWN_UNITS)]
    units += two(wk)
    units += [wv.reshape(KT_D, P, 256).transpose(1, 0, 2).reshape(P, UNIT)]
    units += two(wq) + two(wo)
    w_expert = np.empty((NE, NCH, 3, P, UNIT), np.float32)
    gu = np.stack([f["w_e_gate"][0], f["w_e_up"][0]], axis=2)
    gu = gu.reshape(NE, 2, 4, P, 2, NCH, CH)
    w_expert[:, :, 0:2] = gu.transpose(0, 5, 1, 3, 2, 4, 6).reshape(NE, NCH, 2, P, UNIT)
    dn = f["w_e_down"][0].reshape(NE, NCH, 2, P, D)
    w_expert[:, :, 2] = dn.transpose(0, 1, 3, 2, 4).reshape(NE, NCH, P, UNIT)
    state = np.zeros((P, KT_D, NB, DS + CW - 1), np.float32)
    state[..., :CW - 1] = f["state_conv"][0].reshape(NB, CW - 1, KT_D, P).transpose(3, 2, 0, 1)
    kc = np.zeros((P, 2, NB, WIN + DS), np.float32)
    kc[..., :WIN] = f["cache_k_win"].reshape(NB, WIN, 2, P).transpose(3, 2, 0, 1)
    vc = f["cache_v_win"].reshape(NB, WIN, 256).transpose(1, 0, 2)
    con, buckets = _constants()
    relb = np.concatenate([f["rel_bias"], np.ones((1, NH), np.float32)])
    w_dw = f["w_dw"][0].reshape(CW, KT_D, P).transpose(2, 1, 0)
    return dict(x=x, vec=vec, w_dw=w_dw, con=con, relb=relb, buckets=buckets, state=state, kc=kc, vc=vc,
                w_dense=np.stack(units), w_expert=w_expert.reshape(NE, UPE, P, UNIT))


OUTS = {"y": [P, KT_D, T], "conv_p": [P, KT_D, CW - 1], "conv_s": [P, KT_D, NB, DS + CW - 1],
        "k_p": [P, 2, WIN], "k_s": [P, 2, NB, WIN + DS], "v_p": [WIN, 256], "v_s": [NB, WIN, 256]}


def kernel(**inputs):
    import concourse.bacc as bacc
    from concourse.bass_utils import run_bass_kernel_spmd

    nc = bacc.Bacc("TRN2", target_bir_lowering=False, num_devices=1)
    arrays = {f"in_{n}": np.ascontiguousarray(a) for n, a in _layout(inputs).items()}
    io = {n[3:]: nc.dram_tensor(n, list(a.shape), F32, kind="ExternalInput").ap() for n, a in arrays.items()}
    for n, shape in OUTS.items():
        io[n] = nc.dram_tensor(f"out_{n}", shape, F32, kind="ExternalOutput").ap()
    io["rel_rows"] = nc.dram_tensor("rel_rows", [NH * P * RLEN], F32, kind="Internal").ap()
    build(nc, io)
    r = run_bass_kernel_spmd(nc, [arrays], core_ids=[0]).results[0]
    o = {n: np.asarray(r[f"out_{n}"]) for n in OUTS}
    y = o["y"].transpose(2, 1, 0).reshape(T, D)
    chan = lambda a: np.moveaxis(a, (0, 1), (-1, -2)).reshape(*a.shape[2:], -1)
    k_p = chan(o["k_p"]).reshape(1, WIN, NKV, HD)
    k_s = chan(o["k_s"])[:, DS:].reshape(NB, WIN, NKV, HD)
    return (y[:SEQ].reshape(1, SEQ, D), y[SEQ:].reshape(NB, DS, D),
            chan(o["conv_p"]).reshape(1, 1, CW - 1, D), chan(o["conv_s"])[:, DS:].reshape(1, NB, CW - 1, D),
            k_p, k_s, o["v_p"].reshape(1, WIN, NKV, HD), o["v_s"].reshape(NB, WIN, NKV, HD))
```
